# Optimizing a Trainium2 kernel written in Bass

```python
import math
import jax, jax.numpy as jnp
from jax import lax
import numpy as np

D_MODEL = 1024
BATCH = 1
SEQ = 256
DEPTH = 2

CHUNK = 64
Q_BLOCK = 128
ROPE_THETA = 10000.0
NORM_EPS = 1e-6

N_EVEN = (DEPTH + 1) // 2
N_ODD = DEPTH // 2

A_HEADS = D_MODEL // 128
A_HEAD_DIM = 64
A_LEFT_CHUNKS = 8
A_BAND = (A_LEFT_CHUNKS + 1) * CHUNK
A_MAX_REL = 256
A_WIDTH = A_HEADS * A_HEAD_DIM

B_HEADS = D_MODEL // 128
B_NOPE_DIM = 64
B_ROPE_DIM = 32
B_V_DIM = 64
B_Q_LORA = D_MODEL // 4
B_KV_LORA = D_MODEL // 8
B_WIDTH = B_HEADS * B_V_DIM

EVEN_IN = 3 * A_WIDTH + B_Q_LORA + B_KV_LORA + B_ROPE_DIM
EVEN_MIX = A_WIDTH + B_WIDTH

C_HEAD_DIM = 64
C_HEADS = D_MODEL // (2 * C_HEAD_DIM)
C_WIDTH = C_HEADS * 2 * C_HEAD_DIM

FF_DENSE = 2816
N_EXPERTS = 8
TOP_K = 2
FF_EXPERT = 3584

kernel_name = "hybrid_chunk_causal_relpos_mla_diffattn_moe"

def rms_norm(x, g, eps=NORM_EPS):
    x32 = x.astype(jnp.float32)
    y = x32 * lax.rsqrt(jnp.mean(x32 * x32, axis=-1, keepdims=True) + eps)
    return (y * g.astype(jnp.float32)).astype(x.dtype)

def rope_tables(positions, dim):
    inv_freq = 1.0 / jnp.power(ROPE_THETA, jnp.arange(0, dim, 2, dtype=jnp.float32) / dim)
    ang = positions.astype(jnp.float32)[..., None] * inv_freq
    return jnp.cos(ang), jnp.sin(ang)

def apply_rope(x, cos, sin):
    x1, x2 = jnp.split(x, 2, axis=-1)
    c = cos[:, None].astype(x.dtype)
    s = sin[:, None].astype(x.dtype)
    return jnp.concatenate([x1 * c - x2 * s, x1 * s + x2 * c], axis=-1)

def to_heads(t, n_heads):
    b, s, _ = t.shape
    return t.reshape(b, s, n_heads, -1).transpose(0, 2, 1, 3)

def from_heads(t):
    b, h, s, d = t.shape
    return t.transpose(0, 2, 1, 3).reshape(b, s, h * d)

def chunk_causal_mask(start, seq):
    q_chunk = (start + jnp.arange(Q_BLOCK)) // CHUNK
    k_chunk = jnp.arange(seq) // CHUNK
    return k_chunk[None, :] <= q_chunk[:, None]

def masked_softmax(s, mask):
    s = jnp.where(mask, s.astype(jnp.float32), -jnp.inf)
    return jax.nn.softmax(s, axis=-1)

def sweep_query_blocks(block_fn, qs):
    b, h, s, _ = qs[0].shape
    nb = s // Q_BLOCK
    blocked = tuple(q.reshape(b, h, nb, Q_BLOCK, q.shape[-1]).transpose(2, 0, 1, 3, 4) for q in qs)
    starts = jnp.arange(nb, dtype=jnp.int32) * Q_BLOCK
    out = lax.map(lambda args: block_fn(args[0], *args[1:]), (starts,) + blocked)
    return out.transpose(1, 2, 0, 3, 4).reshape(b, h, s, out.shape[-1])

def chunked_relpos_attention(q, k, v, rel_bias):
    b, h, s, dh = q.shape
    nc = s // CHUNK
    qc = q.reshape(b, h, nc, CHUNK, dh)
    pad = ((0, 0), (0, 0), (A_LEFT_CHUNKS * CHUNK, 0), (0, 0))
    kp = jnp.pad(k, pad).reshape(b, h, nc + A_LEFT_CHUNKS, CHUNK, dh)
    vp = jnp.pad(v, pad).reshape(b, h, nc + A_LEFT_CHUNKS, CHUNK, dh)
    kb = jnp.concatenate([kp[:, :, w:w + nc] for w in range(A_LEFT_CHUNKS + 1)], axis=3)
    vb = jnp.concatenate([vp[:, :, w:w + nc] for w in range(A_LEFT_CHUNKS + 1)], axis=3)
    rel = A_LEFT_CHUNKS * CHUNK + jnp.arange(CHUNK)[:, None] - jnp.arange(A_BAND)[None, :]
    rel = jnp.clip(rel, -A_MAX_REL, A_MAX_REL) + A_MAX_REL
    bias = rel_bias[:, rel].astype(jnp.float32)
    key_chunk = jnp.arange(nc)[:, None] - A_LEFT_CHUNKS + (jnp.arange(A_BAND) // CHUNK)[None, :]
    valid = key_chunk >= 0
    sc = jnp.einsum('bhnqd,bhnkd->bhnqk', qc, kb).astype(jnp.float32) * (dh ** -0.5) + bias[:, None]
    p = masked_softmax(sc, valid[:, None, :])
    o = jnp.einsum('bhnqk,bhnkd->bhnqd', p.astype(v.dtype), vb)
    return o.reshape(b, h, s, dh)

def mla_attention(c_q, c_kv, k_rope_raw, cos, sin, q_norm_g, w_uq, kv_norm_g, w_ukv):
    b, s, _ = c_q.shape
    q = to_heads(rms_norm(c_q, q_norm_g) @ w_uq, B_HEADS)
    q_nope, q_rope = q[..., :B_NOPE_DIM], q[..., B_NOPE_DIM:]
    kv = to_heads(rms_norm(c_kv, kv_norm_g) @ w_ukv, B_HEADS)
    k_nope, v = kv[..., :B_NOPE_DIM], kv[..., B_NOPE_DIM:]
    q_rope = apply_rope(q_rope, cos, sin)
    k_rope = apply_rope(k_rope_raw[:, None], cos, sin)
    q_full = jnp.concatenate([q_nope, q_rope], axis=-1)
    k_full = jnp.concatenate([k_nope, jnp.broadcast_to(k_rope, (b, B_HEADS, s, B_ROPE_DIM))], axis=-1)
    scale = (B_NOPE_DIM + B_ROPE_DIM) ** -0.5

    def block(start, qb):
        sc = jnp.einsum('bhqd,bhkd->bhqk', qb, k_full) * scale
        p = masked_softmax(sc, chunk_causal_mask(start, s))
        return jnp.einsum('bhqk,bhkd->bhqd', p.astype(v.dtype), v)

    return sweep_query_blocks(block, (q_full,))

def diff_attention(q, k, v, cos, sin, lam_q1, lam_k1, lam_q2, lam_k2, subln_g, lambda_init):
    s = q.shape[2]
    q1, q2 = jnp.split(q, 2, axis=-1)
    k1, k2 = jnp.split(k, 2, axis=-1)
    q1, q2 = apply_rope(q1, cos, sin), apply_rope(q2, cos, sin)
    k1, k2 = apply_rope(k1, cos, sin), apply_rope(k2, cos, sin)
    f32 = jnp.float32
    lam = (jnp.exp(jnp.sum(lam_q1.astype(f32) * lam_k1.astype(f32)))
           - jnp.exp(jnp.sum(lam_q2.astype(f32) * lam_k2.astype(f32))) + lambda_init)
    scale = C_HEAD_DIM ** -0.5

    def block(start, q1b, q2b):
        mask = chunk_causal_mask(start, s)
        p1 = masked_softmax(jnp.einsum('bhqd,bhkd->bhqk', q1b, k1) * scale, mask)
        p2 = masked_softmax(jnp.einsum('bhqd,bhkd->bhqk', q2b, k2) * scale, mask)
        a = p1 - lam * p2
        return jnp.einsum('bhqk,bhkd->bhqd', a.astype(v.dtype), v)

    o = sweep_query_blocks(block, (q1, q2))
    return rms_norm(o, subln_g) * (1.0 - lambda_init)

def swiglu(x, w_gu, w_down):
    gate, up = jnp.split(x @ w_gu, 2, axis=-1)
    return (jax.nn.silu(gate) * up) @ w_down

def moe_swiglu(x, w_router, w_gu, w_down):
    b, s, d = x.shape
    t = x.reshape(b * s, d)
    logits = (t @ w_router).astype(jnp.float32)
    top_v, top_i = lax.top_k(logits, TOP_K)
    gates = jax.nn.softmax(top_v, axis=-1)
    combine = jnp.sum(jax.nn.one_hot(top_i, N_EXPERTS, dtype=jnp.float32) * gates[..., None], axis=1)
    y = jnp.zeros_like(t)
    for e in range(N_EXPERTS):
        y = y + combine[:, e:e + 1].astype(t.dtype) * swiglu(t, w_gu[e], w_down[e])
    return y.reshape(b, s, d)

def diff_lambda_init(layer):
    return 0.8 - 0.6 * math.exp(-0.3 * layer)

def setup_inputs(seed: int = 0) -> dict:
    key = jax.random.key(seed)
    ks = iter(jax.random.split(key, 32))
    f32 = jnp.float32

    def w(shape, fan_in):
        return jax.random.normal(next(ks), shape, f32) * (fan_in ** -0.5)

    def gain(shape):
        return 1.0 + 0.02 * jax.random.normal(next(ks), shape, f32)

    x = jax.random.normal(next(ks), (BATCH, SEQ, D_MODEL), f32)
    offset = jax.random.randint(next(ks), (BATCH, 1), 0, 16, dtype=jnp.int32) * CHUNK
    positions = (offset + jnp.arange(SEQ, dtype=jnp.int32)[None, :]).astype(jnp.int32)
    return {
        "x": x,
        "positions": positions,
        "mix_norm_g": gain((DEPTH, D_MODEL)),
        "ffn_norm_g": gain((DEPTH, D_MODEL)),
        "w_in_even": w((N_EVEN, D_MODEL, EVEN_IN), D_MODEL),
        "rel_bias_a": 0.5 * jax.random.normal(next(ks), (N_EVEN, A_HEADS, 2 * A_MAX_REL + 1), f32),
        "q_norm_b": gain((N_EVEN, B_Q_LORA)),
        "w_uq_b": w((N_EVEN, B_Q_LORA, B_HEADS * (B_NOPE_DIM + B_ROPE_DIM)), B_Q_LORA),
        "kv_norm_b": gain((N_EVEN, B_KV_LORA)),
        "w_ukv_b": w((N_EVEN, B_KV_LORA, B_HEADS * (B_NOPE_DIM + B_V_DIM)), B_KV_LORA),
        "w_out_even": w((N_EVEN, EVEN_MIX, D_MODEL), EVEN_MIX),
        "w_in_odd": w((N_ODD, D_MODEL, 3 * C_WIDTH), D_MODEL),
        "lambda_q1": 0.1 * jax.random.normal(next(ks), (N_ODD, C_HEAD_DIM), f32),
        "lambda_k1": 0.1 * jax.random.normal(next(ks), (N_ODD, C_HEAD_DIM), f32),
        "lambda_q2": 0.1 * jax.random.normal(next(ks), (N_ODD, C_HEAD_DIM), f32),
        "lambda_k2": 0.1 * jax.random.normal(next(ks), (N_ODD, C_HEAD_DIM), f32),
        "subln_g": gain((N_ODD, 2 * C_HEAD_DIM)),
        "w_out_odd": w((N_ODD, C_WIDTH, D_MODEL), C_WIDTH),
        "w_gu_dense": w((N_EVEN, D_MODEL, 2 * FF_DENSE), D_MODEL),
        "w_down_dense": w((N_EVEN, FF_DENSE, D_MODEL), FF_DENSE),
        "w_router": w((N_ODD, D_MODEL, N_EXPERTS), D_MODEL),
        "w_gu_moe": w((N_ODD, N_EXPERTS, D_MODEL, 2 * FF_EXPERT), D_MODEL),
        "w_down_moe": w((N_ODD, N_EXPERTS, FF_EXPERT, D_MODEL), FF_EXPERT),
        "final_norm_g": gain((D_MODEL,)),
    }

def reference(x, positions, mix_norm_g, ffn_norm_g, w_in_even, rel_bias_a, q_norm_b, w_uq_b,
              kv_norm_b, w_ukv_b, w_out_even, w_in_odd, lambda_q1, lambda_k1, lambda_q2,
              lambda_k2, subln_g, w_out_odd, w_gu_dense, w_down_dense, w_router, w_gu_moe,
              w_down_moe, final_norm_g):
    cos_b, sin_b = rope_tables(positions, B_ROPE_DIM)
    cos_c, sin_c = rope_tables(positions, C_HEAD_DIM)
    h = x
    for layer in range(DEPTH):
        i = layer // 2
        hn = rms_norm(h, mix_norm_g[layer])
        if layer % 2 == 0:
            proj = hn @ w_in_even[i]
            o1 = A_WIDTH
            o2 = o1 + A_WIDTH
            o3 = o2 + A_WIDTH
            o4 = o3 + B_Q_LORA
            o5 = o4 + B_KV_LORA
            qa = to_heads(proj[..., :o1], A_HEADS)
            ka = to_heads(proj[..., o1:o2], A_HEADS)
            va = to_heads(proj[..., o2:o3], A_HEADS)
            out_a = chunked_relpos_attention(qa, ka, va, rel_bias_a[i])
            out_b = mla_attention(proj[..., o3:o4], proj[..., o4:o5], proj[..., o5:], cos_b, sin_b,
                                  q_norm_b[i], w_uq_b[i], kv_norm_b[i], w_ukv_b[i])
            mix = jnp.concatenate([from_heads(out_a), from_heads(out_b)], axis=-1)
            h = h + mix @ w_out_even[i]
            h = h + swiglu(rms_norm(h, ffn_norm_g[layer]), w_gu_dense[i], w_down_dense[i])
        else:
            qkv = hn @ w_in_odd[i]
            qc = to_heads(qkv[..., :C_WIDTH], C_HEADS)
            kc = to_heads(qkv[..., C_WIDTH:2 * C_WIDTH], C_HEADS)
            vc = to_heads(qkv[..., 2 * C_WIDTH:], C_HEADS)
            out_c = diff_attention(qc, kc, vc, cos_c, sin_c, lambda_q1[i], lambda_k1[i],
                                   lambda_q2[i], lambda_k2[i], subln_g[i], diff_lambda_init(layer))
            h = h + from_heads(out_c) @ w_out_odd[i]
            h = h + moe_swiglu(rms_norm(h, ffn_norm_g[layer]), w_router[i], w_gu_moe[i], w_down_moe[i])
    return rms_norm(h, final_norm_g)


_drawn_inputs = setup_inputs


def setup_inputs(seed=0):
    import zlib

    import numpy as np

    out = dict(_drawn_inputs(seed))
    spreads = {}
    factors = {'q_norm_b': 6.061, 'lambda_q2': 8.0, 'subln_g': 2.889, 'final_norm_g': 2.889}
    for name, (base, spread) in spreads.items():
        noise = np.random.default_rng([zlib.crc32(name.encode()), seed]).standard_normal(out[name].shape)
        drawn = base * np.exp(spread * noise) if base else spread * noise
        out[name] = __import__('jax').numpy.asarray(drawn.astype(out[name].dtype))
    for name, factor in factors.items():
        out[name] = (out[name] * factor).astype(out[name].dtype)
    return out
```

```python
import concourse.bass as bass
from concourse import mybir
from contextlib import ExitStack
import numpy as np

P = 128
D = 1024
S = 256
TT = S // P
KB = D // P
EVEN_IN = 1952
A_HEADS, A_DH, A_REL = 8, 64, 513
B_HEADS, B_NOPE, B_ROPE, B_V = 8, 64, 32, 64
B_QK = B_NOPE + B_ROPE
B_QL, B_KVL = 256, 128
C_HEADS, C_DH, C_DV = 8, 64, 128
FF_DENSE = 2816
N_EXP, FF_EXP = 8, 3584
EPS = 1e-6
NEG = -1.0e30
A_SCALE = A_DH ** -0.5
B_SCALE = B_QK ** -0.5
C_SCALE = C_DH ** -0.5
LAMBDA_INIT = 0.8 - 0.6 * float(np.exp(-0.3))
CH = 512
MAX_PASS = N_EXP + 3

C_ID, C_TRI, C_ONES, C_IOTA = 0, 128, 256, 384
C_MASK, C_FREQ, C_E8, C_R8 = 512, 576, 624, 632
C_COLS = 640
N_FREQ = 48

RAW, SPLIT = 6, 3
T_IN0, T_UQ, T_UKV, T_IN0V, T_OUT0 = 0, 6, 7, 8, 10
T_FFN = 14
N_FULL = FF_DENSE // CH
T_IN1 = T_FFN + 6 * N_FULL + 3
T_OUT1 = T_IN1 + 12
T_MOE = T_OUT1 + 4
M_CH = FF_EXP // CH
M_TILES = 6 * M_CH
IN0_ORDER = [3, 0, 1, 2]
TWO_PI = 2 * float(np.pi)
TURN_PARTS = (6.28125, 0.0019340515136718750, TWO_PI - 6.28125 - 0.0019340515136718750)
ROUND = 1.5 * 2.0 ** 23
SIN_MAX = 3.1415925


def build(nc, a):
    F, R, I32 = mybir.dt.float32, mybir.dt.float32r, mybir.dt.int32
    ALU, ACT, AX = mybir.AluOpType, mybir.ActivationFunctionType, mybir.AxisListType
    ds = bass.ds

    w_in0 = a["w_in_even"][0].rearrange("(k p) n -> p k n", p=P)
    w_uq = a["w_uq_b"][0].rearrange("(k p) n -> p k n", p=P)
    w_ukv = a["w_ukv_b"][0]
    w_out0 = a["w_out_even"][0].rearrange("(k p) n -> p k n", p=P)
    w_gu = a["w_gu_dense"][0].rearrange("(k p) n -> p k n", p=P)
    w_dn = a["w_down_dense"][0].rearrange("(k p) n -> p k n", p=P)
    w_in1 = a["w_in_odd"][0].rearrange("(k p) n -> p k n", p=P)
    w_out1 = a["w_out_odd"][0].rearrange("(k p) n -> p k n", p=P)
    e_gu = a["w_gu_moe"][0].rearrange("e (k p) n -> e p k n", p=P)
    e_dn = a["w_down_moe"][0].rearrange("e (k p) n -> e p k n", p=P)

    ctx = ExitStack()
    with ctx:
        def sb(name, shape, dt=F, where=ctx):
            return where.enter_context(nc.sbuf_tensor(name, shape, dt))

        def sem(name):
            return ctx.enter_context(nc.semaphore(name))

        raw = [sb(f"raw{i}", [P, 2048]) for i in range(RAW)]
        whi = [sb(f"whi{i}", [P, 2048], R) for i in range(SPLIT)]
        wlo = [sb(f"wlo{i}", [P, 2048], R) for i in range(SPLIT)]
        h = sb("h", [P, TT, D])
        gain = [sb(f"gain{i}", [P, D]) for i in range(2)]
        consts = sb("consts_sb", [P, C_COLS])
        small_g = sb("small_g", [P, B_QL + B_KVL + C_DV])
        lam_in = sb("lam_in", [P, 4, C_DH])
        xn = sb("xn", [P, TT, D])
        pos_i = sb("pos_i", [P, TT], I32)
        pos_f = sb("pos_f", [P, TT])
        trig = sb("trig", [P, 4, TT, N_FREQ])
        cc = sb("cc", [P, TT, C_DH])
        ss = sb("ss", [P, TT, C_DH])
        minus_half = sb("minus_half", [P, 32])
        ssq = sb("ssq", [P, 32])
        ms = sb("ms", [P, 32])
        rstd = sb("rstd", [P, 32])
        lam = sb("lam", [P, 8])
        mx = sb("mx", [P, 24, 4])
        nmx = sb("nmx", [P, 24, 4])
        den = sb("den", [P, 24, 4])
        rden = sb("rden", [P, 24, 4])
        wr = sb("wr", [P, KB, N_EXP])
        wrhi = sb("wrhi", [P, KB, N_EXP], R)
        wrlo = sb("wrlo", [P, KB, N_EXP], R)
        ident = consts[:, C_ID:C_ID + P]
        tri = consts[:, C_TRI:C_TRI + P]
        ones = consts[:, C_ONES:C_ONES + P]
        iota = consts[:, C_IOTA:C_IOTA + P]
        mask = consts[:, C_MASK:C_MASK + 64]
        e8 = consts[:, C_E8:C_E8 + 8]
        r8 = consts[:, C_R8:C_R8 + 8]
        gq, gkv = small_g[:, 0:B_QL], small_g[:, B_QL:B_QL + B_KVL]
        g_sub = small_g[:, B_QL + B_KVL:]

        with ExitStack() as reuse:
            xhi = sb("xhi", [P, KB, S], R, reuse)
            xlo = sb("xlo", [P, KB, S], R, reuse)
        with ExitStack() as reuse:
            qT = sb("qT", [P, KB, S], F, reuse)
            kT = sb("kT", [P, KB, S], F, reuse)
        hold = ctx.enter_context(nc.sbuf_tensor("hold_x", [P, 2 * KB * S], F))

        with ExitStack() as reuse:
            proj = sb("proj", [P, TT, EVEN_IN], F, reuse)
            qB = sb("qB", [P, TT, B_HEADS, B_QK], F, reuse)
            kB = sb("kB", [P, TT, B_HEADS, B_QK], F, reuse)
            vB = sb("vB", [P, TT, B_HEADS, B_V], F, reuse)
            qTA = sb("qTA", [P, 4, S], F, reuse)
            kTA = sb("kTA", [P, 4, S], F, reuse)
            bias = sb("bias", [P, A_HEADS, S], F, reuse)
            with ExitStack() as again:
                lat = sb("lat", [P, TT, B_QL + B_KVL], F, again)
                lhi = sb("lhi", [P, 3, S], R, again)
                llo = sb("llo", [P, 3, S], R, again)
                ropeB = sb("ropeB", [P, 4, TT, 16], F, again)
                ropeQ = sb("ropeQ", [P, 4, B_HEADS, 16], F, again)
            biased = [sb(f"biased{i}", [P, 384], F, reuse) for i in range(2)]
            probs = [sb(f"probs{i}", [P, 384], F, reuse) for i in range(2)]
            probsT = [sb(f"probsT{i}", [P, 384], F, reuse) for i in range(2)]
        with ExitStack() as reuse:
            act_g = sb("act_g", [P, TT, CH], F, reuse)
            hid = sb("hid", [P, TT, CH], F, reuse)
            hidhi = sb("hidhi", [P, 4, S], R, reuse)
            hidlo = sb("hidlo", [P, 4, S], R, reuse)
        with ExitStack() as reuse:
            proj1 = sb("proj1", [P, TT, 3 * D], F, reuse)
            qTC = sb("qTC", [P, KB, S], F, reuse)
            kTC = sb("kTC", [P, KB, S], F, reuse)
            rot = [sb(f"rot{i}", [P, CH], F, reuse) for i in range(2)]
            probs1 = [sb(f"probs1_{i}", [P, 2, 384], F, reuse) for i in range(2)]
            scaled2 = sb("scaled2", [P, 384], F, reuse)
            diff = [sb(f"diff{i}", [P, 384], F, reuse) for i in range(2)]
            diffT = [sb(f"diffT{i}", [P, 384], F, reuse) for i in range(2)]
            junk = sb("junk", [P, TT, C_DV], F, reuse)
        with ExitStack() as reuse:
            thi = sb("thi", [P, TT, D], R, reuse)
            tlo = sb("tlo", [P, TT, D], R, reuse)
            xghi = sb("xghi", [P, KB, P], R, reuse)
            xglo = sb("xglo", [P, KB, P], R, reuse)
            act_e = sb("act_e", [P, CH], F, reuse)
            hid_e = sb("hid_e", [P, CH], F, reuse)
            hehi = sb("hehi", [P, 4, P], R, reuse)
            helo = sb("helo", [P, 4, P], R, reuse)
            yhi = sb("yhi", [P, D], R, reuse)
            ylo = sb("ylo", [P, D], R, reuse)
            sel = sb("sel", [P, TT, P], R, reuse)
            selT = sb("selT", [P, S], R, reuse)
            gcur = sb("gcur", [P, TT], F, reuse)
            gslot = sb("gslot", [P, 1], F, reuse)
            logit = sb("logit", [P, TT, 8], F, reuse)
            rt = sb("rt", [P, 16, TT, 8], F, reuse)
            rs = sb("rs", [P, 16, TT], F, reuse)
            scan = sb("scan", [P, 4, 16], F, reuse)
            chosen = sb("chosen", [P, TT, 12], F, reuse)
            slot = sb("slot", [P, TT, 12], F, reuse)
            gate = sb("gate", [P, TT, 12], F, reuse)
            order = sb("order", [P, 16], F, reuse)
            order_i = sb("order_i", [P, 16], I32, reuse)

        ps = ctx.enter_context(nc.psum_tensor("ps", [P, 8, CH], F))

        s_x = sem("x_loaded")
        s_consts, s_small, s_bias_in, s_lam_in, s_wr_in, s_pos = [sem(n) for n in (
            "consts_loaded", "small_gains_loaded", "bias_loaded", "lambda_loaded", "router_loaded", "positions_loaded")]
        s_gain = [sem(f"gain_loaded{i}") for i in range(2)]
        s_raw = [sem(f"raw_loaded{i}") for i in range(RAW)]
        s_hi, s_lo, s_used = sem("hi_ready"), sem("lo_ready"), sem("tile_used")
        full = [sem(f"bank_full{i}") for i in range(8)]
        free = [sem(f"bank_free{i}") for i in range(8)]
        s_sq, s_ms, s_rstd, s_xn = [sem(n) for n in ("squares_summed", "mean_ready", "rstd_ready", "normed")]
        s_hiT, s_loT = sem("left_hi_ready"), sem("left_lo_ready")
        s_dve, s_pool, s_const = sem("vector_step"), sem("pool_step"), sem("exponent_set")
        s_lat, s_rope, s_bias = [sem(n) for n in ("latents_normed", "rotated_b", "bias_masked")]
        s_trig, s_sin, s_lam = sem("angles_ready"), sem("sines_ready"), sem("lambda_terms")
        s_sc, s_nm, s_exp, s_diff = [sem(n) for n in ("scores_full", "maxima_ready", "exponentials_ready", "difference_ready")]
        s_ptf, s_pT, s_of, s_mix = [sem(n) for n in ("probsT_full", "probsT_ready", "head_full", "head_out")]
        s_rot, s_sqc, s_sub = sem("rotated_c"), sem("head_squares"), sem("heads_normed")
        s_res = sem("residual_added")
        f_act, f_h, f_t, f_hhi, f_ht, f_d, f_add = [sem(n) for n in (
            "ffn_silu", "ffn_hidden", "ffn_hidT_full", "ffn_hidT_hi", "ffn_hidT_ready", "ffn_down_full", "ffn_down_added")]
        s_wr, s_log, s_dlt, s_ex, s_cho, s_rank, s_order = [sem(n) for n in (
            "router_split", "logits_full", "second_minus_first", "second_exp", "choice_ready", "ranks_full", "passes_ready")]
        s_tok, s_tlo = sem("tokens_hi"), sem("tokens_split")
        m_sel, m_aux, m_auxr, m_x, m_xhi, m_xlo, m_act, m_h, m_t, m_thi, m_tr, m_yhi, m_ylo, m_acc, m_add = [
            sem(n) for n in (
                "selection_ready", "selT_full", "selT_ready", "gather_full", "gather_hi", "gather_ready",
                "silu_ready", "hidden_ready", "hidT_full", "hidT_hi", "hidT_ready",
                "expert_out_hi", "expert_out_ready", "scatter_full", "scatter_added")]
        s_fin, s_out = sem("final_normed"), sem("stored")

        use, uses, fulls = {}, [0] * 8, [0] * 8

        def plan(key, bank, counted=True):
            use[key] = (bank, fulls[bank], uses[bank])
            fulls[bank] += 1
            uses[bank] += counted

        def plan_left(stage):
            for g in range(4):
                plan(("left", stage, g), 4 + g % 2, counted=False)

        def plan_columns(stage, c, pair):
            for t in range(TT):
                plan((stage, c, t), 2 * pair + t, counted=stage[:3] != "out")

        def plan_heads(name, groups):
            for g in range(groups):
                plan((name, g), 4 + g % 2)

        UNITS0, UNITS = A_HEADS + B_HEADS, A_HEADS + B_HEADS + C_HEADS
        plan_left(0)
        plan_columns("in0", 3, 0)
        plan_columns("in0", 0, 1)
        plan("lat0", 4, counted=False)
        plan("lat1", 5, counted=False)
        plan_columns("in0", 1, 0)
        plan_columns("uq", 0, 1)
        plan_columns("uq", 1, 0)
        plan_columns("ukv", 0, 1)
        plan_columns("ukv", 1, 0)
        plan_heads("qA", 2)
        plan_heads("kA", 2)
        plan_columns("in0", 2, 1)
        plan_heads("qB", 4)
        plan_heads("kB", 4)
        before_units0 = list(uses)
        plan_left(1)
        plan_columns("out0", 0, 0)
        plan_columns("out0", 1, 1)
        plan_left(2)
        before_ffn = list(uses)
        plan_left(3)
        for c in range(6):
            plan_columns("in1", c, c % 2)
            if c == 2:
                plan_heads("qC", 4)
            if c == 4:
                plan_heads("kC", 4)
        before_units1 = list(uses)
        plan_left(4)
        plan_columns("out1", 0, 0)
        plan_columns("out1", 1, 1)
        plan_left(5)
        before_moe = list(uses)

        def wait_full(eng, key):
            eng.wait_ge(full[use[key][0]], use[key][1] + 1)

        def wait_free(eng, key):
            eng.wait_ge(free[use[key][0]], use[key][2] + 1)

        def bank(key):
            return ps[:, use[key][0], :]

        def spread(ap, shape, axis):
            return ap.unsqueeze(axis).to_broadcast(shape)

        def raw_count(n):
            return 16 * (n // RAW + 1)

        def width_of(n):
            return {0: 1664, 1: 1664, T_UQ: 1536, T_UKV: 1024}.get(n, 2048)

        MIX0, FFN0, MIX1, FFN1, FINAL = range(5)
        LAT, SUBLN = 10, 16
        SQ = {MIX0: 2, FFN0: 8, MIX1: 10, FFN1: 12, FINAL: 14}
        LEFT = {0: 4, 1: 10, 2: 14, 3: 18, 4: 22, 5: 26}
        LAST = N_FULL
        T_LAST = T_FFN + 6 * N_FULL - 2
        block = ctx.enter_context(nc.Block())

        @block.sync
        def _(sp):
            for t in range(TT):
                sp.dma_start(h[:, t, :], a["x"][0, t * P:(t + 1) * P, :]).then_inc(s_x, 16)

            def load(n, dst_shape, src):
                if n >= RAW:
                    sp.wait_ge(s_lo, n - RAW + 1)
                k, m = dst_shape
                dst = raw[n % RAW][:, 0:k * m].rearrange("p (k m) -> p k m", k=k)
                sp.dma_start(dst, src).then_inc(s_raw[n % RAW], 16)

            for i, c in enumerate(IN0_ORDER[:3]):
                width = min(CH, EVEN_IN - c * CH)
                for b in range(2):
                    load(T_IN0 + 2 * i + b, (4, width), w_in0[:, 4 * b:4 * b + 4, c * CH:c * CH + width])
            load(T_UQ, (2, 768), w_uq)
            load(T_UKV, (1, D), w_ukv.rearrange("p (k n) -> p k n", k=1))
            for b in range(2):
                load(T_IN0V + b, (4, CH), w_in0[:, 4 * b:4 * b + 4, 2 * CH:3 * CH])
            for c in range(2):
                for b in range(2):
                    load(T_OUT0 + 2 * c + b, (4, CH), w_out0[:, 4 * b:4 * b + 4, c * CH:(c + 1) * CH])
            for half in range(2):
                for b in range(2):
                    load(T_FFN + 2 * half + b, (4, CH), w_gu[:, 4 * b:4 * b + 4, half * FF_DENSE:half * FF_DENSE + CH])
            with sp.Fori(1, N_FULL) as j:
                for r in range(6):
                    n = T_FFN + 4 + r
                    sp.wait_ge(s_lo, (j - 1) * 6 + (n - RAW + 1))
                    dst = raw[n % RAW][:, :].rearrange("p (k m) -> p k m", k=4)
                    if r < 4:
                        half, b = r // 2, r % 2
                        src = w_gu[:, 4 * b:4 * b + 4, ds(j * CH + half * FF_DENSE, CH)]
                    else:
                        src = w_dn[:, ds(j * 4 - 4, 4), (r - 4) * CH:(r - 3) * CH]
                    sp.dma_start(dst, src).then_inc(s_raw[n % RAW], 16)
            n = T_FFN + 6 * N_FULL - 2
            rest = FF_DENSE - N_FULL * CH
            for half in range(2):
                at = half * FF_DENSE + N_FULL * CH
                load(n + half, (8, rest), w_gu[:, :, at:at + rest])
            for half in range(2):
                load(n + 2 + half, (4, CH), w_dn[:, 4 * N_FULL - 4:4 * N_FULL, half * CH:(half + 1) * CH])
            load(n + 4, (2, D), w_dn[:, 4 * N_FULL:4 * N_FULL + 2, :])
            for c in range(6):
                for b in range(2):
                    load(T_IN1 + 2 * c + b, (4, CH), w_in1[:, 4 * b:4 * b + 4, c * CH:(c + 1) * CH])
            for c in range(2):
                for b in range(2):
                    load(T_OUT1 + 2 * c + b, (4, CH), w_out1[:, 4 * b:4 * b + 4, c * CH:(c + 1) * CH])

            def expert_tiles(first, e):
                def put(i, src):
                    sp.wait_ge(s_lo, first + (i - RAW + 1))
                    n_slot = (T_MOE + i) % RAW
                    dst = raw[n_slot][:, :].rearrange("p (k m) -> p k m", k=4)
                    sp.dma_start(dst, src).then_inc(s_raw[n_slot], 16)

                def gu(half, b, at):
                    return e_gu[ds(e, 1), :, 4 * b:4 * b + 4, ds(at + half * FF_EXP, CH)].rearrange("e p k n -> (e p) k n")

                def dn(k, half):
                    return e_dn[ds(e, 1), :, ds(k, 4), half * CH:(half + 1) * CH].rearrange("e p k n -> (e p) k n")

                for i in range(4):
                    put(i, gu(i // 2, i % 2, 0))
                with sp.Fori(1, M_CH) as j:
                    for r in range(6):
                        sp.wait_ge(s_lo, (j - 1) * 6 + first + (4 + r - RAW + 1))
                        n_slot = (T_MOE + 4 + r) % RAW
                        dst = raw[n_slot][:, :].rearrange("p (k m) -> p k m", k=4)
                        src = gu(r // 2, r % 2, j * CH) if r < 4 else dn(j * 4 - 4, r - 4)
                        sp.dma_start(dst, src).then_inc(s_raw[n_slot], 16)
                for half in range(2):
                    put(M_TILES - 2 + half, dn(4 * M_CH - 4, half))

            expert_tiles(T_MOE, 0)
            sp.wait_ge(s_order, 1)
            passes = sp.value_load(order_i[0:1, 15:16], min_val=N_EXP, max_val=MAX_PASS)
            with sp.Fori(1, passes) as p:
                e = sp.value_load(order_i[0:1, ds(p, 1)], min_val=0, max_val=N_EXP - 1)
                expert_tiles(p * M_TILES + T_MOE, e)
            sp.wait_ge(s_fin, 2)
            for t in range(TT):
                sp.dma_start(a["out"][0, t * P:(t + 1) * P, :], xn[:, t, :]).then_inc(s_out, 16)
            sp.wait_ge(s_out, 16 * TT)

        @block.scalar
        def _(act):
            done = [0]

            def load_gain(k, src):
                if k >= 2:
                    act.wait_ge(s_xn, 2 * (k - 1))
                act.dma_start(gain[k % 2][:], src.to_broadcast([P, D])).then_inc(s_gain[k % 2], 16)

            act.dma_start(consts[:], a["consts"]).then_inc(s_consts, 16)
            load_gain(0, a["mix_norm_g"][0:1, :])
            act.dma_start(small_g[:, 0:B_QL], a["q_norm_b"][0:1, :].to_broadcast([P, B_QL])).then_inc(s_small, 16)
            act.dma_start(small_g[:, B_QL:B_QL + B_KVL],
                          a["kv_norm_b"][0:1, :].to_broadcast([P, B_KVL])).then_inc(s_small, 16)
            act.dma_start(g_sub, a["subln_g"][0:1, :].to_broadcast([P, C_DV])).then_inc(s_small, 16)
            with nc.allow_non_contiguous_dma(reason="256 positions, the router's short rows"):
                act.dma_start(pos_i[:], a["positions"].rearrange("a (t p) -> p (a t)", p=P)).then_inc(s_pos, 16)
                act.dma_start(wr[:], a["w_router"][0].rearrange("(k p) n -> p k n", p=P)).then_inc(s_wr_in, 16)

            def split(n):
                act.wait_ge(s_raw[n % RAW], raw_count(n))
                if n >= SPLIT:
                    act.wait_ge(s_used, n - SPLIT + 1)
                w = width_of(n)
                nc.scalar.activation(whi[n % SPLIT][:, 0:w], raw[n % RAW][:, 0:w], ACT.Copy).then_inc(s_hi, 1)

            def upto(n):
                while done[0] <= n:
                    split(done[0])
                    done[0] += 1

            def squares(k):
                for t in range(TT):
                    nc.scalar.activation(xn[:, t, :], h[:, t, :], ACT.Square,
                                         accum_out=ssq[:, 2 * k + t:2 * k + t + 1]).then_inc(s_sq, 1)

            def left_hi(stage):
                for g in range(4):
                    wait_full(act, ("left", stage, g))
                    nc.scalar.activation(xhi[:, 2 * g:2 * g + 2, :], bank(("left", stage, g)).rearrange(
                        "p (k s) -> p k s", k=2), ACT.Copy).then_inc(s_hiT, 1)

            def copy_out(key, dst, src=None):
                nc.scalar.activation(dst, bank(key) if src is None else src, ACT.Copy).then_inc(free[use[key][0]], 1)

            act.wait_ge(s_x, 16 * TT)
            squares(MIX0)
            for hd in range(A_HEADS):
                row = a["rel_bias_a"][0, hd:hd + 1, P + 1:P + 1 + S]
                act.dma_start(bias[:, hd, :], bass.AP(row.tensor, row.offset, [[1, P], [1, S]])).then_inc(s_bias_in, 16)
            for i, name in enumerate(("lambda_q1", "lambda_k1", "lambda_q2", "lambda_k2")):
                act.dma_start(lam_in[:, i, :], a[name][0:1, :].to_broadcast([P, C_DH])).then_inc(s_lam_in, 16)
            load_gain(1, a["ffn_norm_g"][0:1, :])
            upto(2)
            left_hi(0)
            upto(3)
            act.wait_ge(s_used, T_IN0 + 2)
            for t in range(TT):
                copy_out(("in0", 3, t), proj[:, t, 1536:EVEN_IN], bank(("in0", 3, t))[:, 0:416])
            for t in range(TT):
                wait_free(act, ("in0", 3, t))
            for t in range(TT):
                for c0, c1 in ((0, B_QL), (B_QL, B_QL + B_KVL)):
                    col = LAT + 2 * t + (c0 > 0)
                    nc.scalar.activation(lat[:, t, c0:c1], proj[:, t, 1536 + c0:1536 + c1], ACT.Square,
                                         accum_out=ssq[:, col:col + 1]).then_inc(s_sq, 1)
            upto(5)
            act.wait_ge(s_used, T_IN0 + 4)
            for t in range(TT):
                copy_out(("in0", 0, t), proj[:, t, 0:CH])
            wait_full(act, "lat0")
            nc.scalar.activation(lhi[:, 0:2, :], bank("lat0").rearrange("p (k s) -> p k s", k=2), ACT.Copy).then_inc(s_hiT, 1)
            wait_full(act, "lat1")
            nc.scalar.activation(lhi[:, 2, :], bank("lat1")[:, 0:S], ACT.Copy).then_inc(s_hiT, 1)
            act.wait_ge(s_trig, 2)
            nc.scalar.activation(trig[:, 3, :, :], trig[:, 0, :, :], ACT.Sin).then_inc(s_sin, 1)
            nc.scalar.activation(trig[:, 2, :, :], trig[:, 1, :, :], ACT.Sin).then_inc(s_sin, 1)
            upto(7)
            act.wait_ge(s_used, T_IN0 + 6)
            for t in range(TT):
                copy_out(("in0", 1, t), proj[:, t, CH:2 * CH])
            upto(8)
            act.wait_ge(s_used, T_UQ + 1)
            for c, w in ((0, CH), (1, 768 - CH)):
                for t in range(TT):
                    copy_out(("uq", c, t), qB[:, t, :, :].rearrange("p a b -> p (a b)")[:, c * CH:c * CH + w],
                             bank(("uq", c, t))[:, 0:w])
            upto(9)
            act.wait_ge(s_used, T_UKV + 1)
            for c in range(2):
                for t in range(TT):
                    src = bank(("ukv", c, t)).rearrange("p (a b) -> p a b", a=4)
                    nc.scalar.activation(kB[:, t, 4 * c:4 * c + 4, 0:B_NOPE], src[:, :, 0:B_NOPE], ACT.Copy)
                    copy_out(("ukv", c, t), vB[:, t, 4 * c:4 * c + 4, :], src[:, :, B_NOPE:])
            for name, dst in (("qA", qTA), ("kA", kTA)):
                for g in range(2):
                    wait_full(act, (name, g))
                    copy_out((name, g), dst[:, 2 * g:2 * g + 2, :].rearrange("p k s -> p (k s)"))
            upto(11)
            act.wait_ge(s_used, T_IN0V + 2)
            for t in range(TT):
                copy_out(("in0", 2, t), proj[:, t, 2 * CH:3 * CH])
            for g in range(4):
                wait_full(act, ("qB", g))
                copy_out(("qB", g), qT[0:B_QK, 2 * g:2 * g + 2, :].rearrange("p k s -> p (k s)"),
                         ps[0:B_QK, use[("qB", g)][0], :])
            upto(12)

            def exponentials(u):
                act.wait_ge(s_nm, u + 1)
                if u < UNITS0 and u >= 2:
                    act.wait_ge(s_ptf, u - 1)
                if u >= UNITS0 + 2:
                    act.wait_ge(s_diff, u - UNITS0 - 1)
                for m in range(1 if u < UNITS0 else 2):
                    for t, (c0, c1) in enumerate(((0, 128), (128, 384))):
                        col = 2 * m + t
                        src = biased[u % 2][:, c0:c1] if u < A_HEADS else ps[:, 2 * (u % 2) + m, c0:c1]
                        dst = probs[u % 2][:, c0:c1] if u < UNITS0 else probs1[u % 2][:, m, c0:c1]
                        last = nc.scalar.activation(
                            dst, src, ACT.Exp, bias=nmx[:, u, col:col + 1],
                            scale=1.0 if u < A_HEADS else B_SCALE if u < UNITS0 else C_SCALE,
                            accum_out=den[:, u, col:col + 1])
                last.then_inc(s_exp, 1)

            def probs_out(u, dst):
                act.wait_ge(s_ptf, u + 1)
                if u >= 2:
                    act.wait_ge(s_of, u - 1)
                nc.scalar.activation(dst[u % 2][:, :], ps[:, 4 + u % 2, 0:384], ACT.Copy).then_inc(s_pT, 1)

            exponentials(0)
            for u in range(UNITS0):
                if u + 1 < UNITS0:
                    exponentials(u + 1)
                probs_out(u, probsT)
            left_hi(1)
            upto(15)
            act.wait_ge(s_res, 4)
            squares(FFN0)
            load_gain(MIX1, a["mix_norm_g"][1:2, :])
            left_hi(2)
            upto(T_FFN + 3)

            def silu(j, width):
                nc.scalar.activation(act_g[:, :, 0:width], ps[:, 0:2, 0:width], ACT.Silu).then_inc(f_act, 1)

            def hid_hi(j, k=4):
                act.wait_ge(f_t, j + 1)
                nc.scalar.activation(hidhi[:, 0:k, :], ps[:, 4:6, :].rearrange("p b (k s) -> p (b k) s", k=2)[:, 0:k, :],
                                     ACT.Copy).then_inc(f_hhi, 1)

            act.wait_ge(s_used, T_FFN + 2)
            silu(0, CH)
            upto(T_FFN + 5)
            with act.Fori(1, N_FULL) as j:
                def split_next(r):
                    n = T_FFN + 4 + r
                    act.wait_ge(s_raw[n % RAW], (j - 1) * 16 + raw_count(n))
                    act.wait_ge(s_used, (j - 1) * 6 + (n - SPLIT + 1))
                    nc.scalar.activation(whi[n % SPLIT][:, :], raw[n % RAW][:, :], ACT.Copy).then_inc(s_hi, 1)

                split_next(2)
                split_next(3)
                act.wait_ge(s_used, (j - 1) * 6 + (T_FFN + 6))
                act.wait_ge(f_h, j * 1)
                silu(j, CH)
                hid_hi(j - 1)
                for r in range(4, 8):
                    split_next(r)
            done[0] = T_LAST + 2
            upto(T_LAST + 2)
            act.wait_ge(s_used, T_LAST + 1)
            act.wait_ge(f_h, LAST)
            silu(LAST, 256)
            hid_hi(LAST - 1)
            upto(T_LAST + 5)
            hid_hi(LAST, 2)
            upto(T_LAST + 6)
            act.wait_ge(f_add, 4 * (LAST + 1))
            squares(MIX1)
            load_gain(FFN1, a["ffn_norm_g"][1:2, :])
            left_hi(3)

            act.wait_ge(s_lam, 1)
            nc.scalar.activation(lam[:, 2:4], lam[:, 0:2], ACT.Exp).then_inc(s_lam, 1)
            act.wait_ge(s_wr_in, 16)
            nc.scalar.activation(wrhi[:], wr[:], ACT.Copy).then_inc(s_wr, 1)
            upto(T_IN1 + 7)
            for g in range(4):
                wait_full(act, ("qC", g))
                copy_out(("qC", g), qTC[:, 2 * g:2 * g + 2, :].rearrange("p k s -> p (k s)"))
            upto(T_IN1 + 11)
            act.wait_ge(s_used, T_IN1 + 10)
            for t in range(TT):
                copy_out(("in1", 4, t), proj1[:, t, 4 * CH:5 * CH])
            for g in range(4):
                wait_full(act, ("kC", g))
                copy_out(("kC", g), kTC[:, 2 * g:2 * g + 2, :].rearrange("p k s -> p (k s)"))
            upto(T_IN1 + 13)
            act.wait_ge(s_used, T_IN1 + 12)
            for t in range(TT):
                copy_out(("in1", 5, t), proj1[:, t, 5 * CH:6 * CH])
            upto(T_OUT1 + 2)
            exponentials(UNITS0)
            for u in range(UNITS0, UNITS):
                if u + 1 < UNITS:
                    exponentials(u + 1)
                probs_out(u, diffT)
                for v in ([u - 1] if u > UNITS0 else []) + ([u] if u == UNITS - 1 else []):
                    act.wait_ge(s_mix, v + 1)
                    if v > UNITS0:
                        act.wait_ge(s_sqc, v - UNITS0)
                    for t in range(TT):
                        hd = v - UNITS0
                        col = SUBLN + C_HEADS * t + hd
                        last = nc.scalar.activation(junk[:, t, :], xn[:, t, hd * C_DV:(hd + 1) * C_DV], ACT.Square,
                                                    accum_out=ssq[:, col:col + 1])
                    last.then_inc(s_sqc, 1)
            left_hi(4)
            upto(T_MOE - 1)
            act.wait_ge(s_res, 8)
            squares(FFN1)
            load_gain(FINAL, a["final_norm_g"].rearrange("(a n) -> a n", a=1))
            act.wait_ge(s_xn, 8)
            for t in range(TT):
                nc.scalar.activation(thi[:, t, :], xn[:, t, :], ACT.Copy).then_inc(s_tok, 1)
            left_hi(5)
            act.wait_ge(s_dlt, 1)
            nc.scalar.activation(rs[:, 5, :], rs[:, 4, :], ACT.Exp).then_inc(s_ex, 1)

            act.wait_ge(s_order, 1)
            passes = act.value_load(order_i[0:1, 15:16], min_val=N_EXP, max_val=MAX_PASS)
            with act.Fori(0, passes) as p:
                def split_tile(i, extra=0, turns=0):
                    n = T_MOE + i
                    act.wait_ge(s_raw[n % RAW], p * (16 * M_CH) + turns * 16 + raw_count(n))
                    act.wait_ge(s_used, p * M_TILES + turns * 6 + (n - SPLIT + 1))
                    nc.scalar.activation(whi[n % SPLIT][:, :], raw[n % RAW][:, :], ACT.Copy).then_inc(s_hi, 1)

                def silu_e(j):
                    nc.scalar.activation(act_e[:], ps[:, 0, :], ACT.Silu).then_inc(m_act, 1)

                def hid_hi_e(j):
                    act.wait_ge(m_t, p * M_CH + j + 1)
                    nc.scalar.activation(hehi[:], ps[:, 2, :].rearrange("p (k s) -> p k s", k=4),
                                         ACT.Copy).then_inc(m_thi, 1)

                for i in range(3):
                    split_tile(i)
                act.wait_ge(m_x, p + 1)
                nc.scalar.activation(xghi[:], ps[:, 6:8, :].rearrange("p b (k s) -> p (b k) s", k=4),
                                     ACT.Copy).then_inc(m_xhi, 1)
                split_tile(3)
                act.wait_ge(s_used, p * M_TILES + (T_MOE + 2))
                silu_e(0)
                split_tile(4)
                split_tile(5)
                with act.Fori(1, M_CH) as j:
                    split_tile(6, turns=j - 1)
                    split_tile(7, turns=j - 1)
                    act.wait_ge(s_used, p * M_TILES + j * 6 + T_MOE)
                    act.wait_ge(m_h, p * M_CH + j)
                    silu_e(j)
                    hid_hi_e(j - 1)
                    for i in range(8, 12):
                        split_tile(i, turns=j - 1)
                hid_hi_e(M_CH - 1)
                act.wait_ge(s_used, p * M_TILES + (T_MOE + M_TILES))
                act.wait_ge(m_auxr, p + 1)
                nc.scalar.activation(yhi[:], ps[:, 3:5, :].rearrange("p b n -> p (b n)"), ACT.Copy,
                                     scale=gslot[:, 0:1]).then_inc(m_yhi, 1)
            act.wait_ge(m_add, passes * 4)
            squares(FINAL)

        @block.gpsimd
        def _(pool):
            steps = [0]

            def step(i):
                i.then_inc(s_pool, 1)
                steps[0] += 1

            def settle():
                pool.wait_ge(s_pool, steps[0])

            def rsqrt(count, c0, n):
                pool.wait_ge(s_ms, count)
                pool.tensor_tensor(rstd[:, c0:c0 + n], ms[:, c0:c0 + n], minus_half[:, 0:n], ALU.pow).then_inc(s_rstd, 1)

            pool.memset(minus_half[:], -0.5).then_inc(s_const, 1)
            pool.wait_ge(s_const, 1)
            rsqrt(1, 0, 2)
            pool.wait_ge(s_bias_in, 16 * A_HEADS)
            pool.wait_ge(s_consts, 16)
            pool.tensor_tensor(bias[0:64, :, 0:64], bias[0:64, :, 0:64],
                               spread(mask[0:64, :], [64, A_HEADS, 64], 1), ALU.add).then_inc(s_bias, 1)
            rsqrt(2, LAT, 4)
            pool.wait_ge(s_sin, 2)
            for half in range(2):
                cols = slice(32 * half, 32 * half + 32)
                step(pool.tensor_copy(cc[:, :, cols], trig[:, 2, :, 16:48]))
                step(pool.tensor_scalar(ss[:, :, cols], trig[:, 3, :, 16:48], 2.0 * half - 1.0, None, ALU.mult))
            settle()
            for t in range(TT):
                wait_free(pool, ("in0", 3, t))
            x1, x2 = proj[:, :, 1920:1936], proj[:, :, 1936:1952]
            cos, sin = trig[:, 2, :, 0:16], trig[:, 3, :, 0:16]
            for i, (x, y) in enumerate(((x1, cos), (x2, sin), (x1, sin), (x2, cos))):
                step(pool.tensor_tensor(ropeB[:, i, :, :], x, y, ALU.mult))
            settle()
            step(pool.tensor_tensor(ropeB[:, 0, :, :], ropeB[:, 0, :, :], ropeB[:, 1, :, :], ALU.subtract))
            step(pool.tensor_tensor(ropeB[:, 2, :, :], ropeB[:, 2, :, :], ropeB[:, 3, :, :], ALU.add))
            settle()
            for t in range(TT):
                for half in range(2):
                    at = B_NOPE + 16 * half
                    pool.tensor_copy(kB[:, t, :, at:at + 16],
                                     spread(ropeB[:, 2 * half, t, :], [P, B_HEADS, 16], 1)).then_inc(s_rope, 1)
            for c in range(2):
                for t in range(TT):
                    wait_free(pool, ("uq", c, t))
            for t in range(TT):
                x1, x2 = qB[:, t, :, 64:80], qB[:, t, :, 80:96]
                c, s = [spread(trig[:, i, t, 0:16], [P, B_HEADS, 16], 1) for i in (2, 3)]
                for i, (x, y) in enumerate(((x1, c), (x2, s), (x1, s), (x2, c))):
                    step(pool.tensor_tensor(ropeQ[:, i, :, :], x, y, ALU.mult))
                settle()
                pool.tensor_tensor(x1, ropeQ[:, 0, :, :], ropeQ[:, 1, :, :], ALU.subtract).then_inc(s_rope, 1)
                pool.tensor_tensor(x2, ropeQ[:, 2, :, :], ropeQ[:, 3, :, :], ALU.add).then_inc(s_rope, 1)
                pool.wait_ge(s_rope, 4 + 2 * (t + 1))
            rsqrt(3, 2 * FFN0, 2)
            rsqrt(4, 2 * MIX1, 2)
            rsqrt(5, SUBLN, 16)
            rsqrt(6, 2 * FFN1, 2)
            rsqrt(7, 2 * FINAL, 2)

        @block.vector
        def _(dve):
            done, steps = [0], [0]

            def step(i):
                i.then_inc(s_dve, 1)
                steps[0] += 1

            def settle():
                dve.wait_ge(s_dve, steps[0])

            def upto(n):
                while done[0] <= n:
                    m = done[0]
                    dve.wait_ge(s_hi, m + 1)
                    w = width_of(m)
                    dve.tensor_tensor(wlo[m % SPLIT][:, 0:w], raw[m % RAW][:, 0:w], whi[m % SPLIT][:, 0:w].bitcast(F),
                                      ALU.subtract).then_inc(s_lo, 1)
                    done[0] += 1

            def mean(c0, n, width, stride=1):
                return dve.tensor_scalar(ms[:, c0:c0 + n * stride:stride], ssq[:, c0:c0 + n * stride:stride],
                                         1.0 / width, EPS, ALU.mult, ALU.add)

            def norm(k, count, out=None):
                dve.wait_ge(s_sq, SQ[k])
                mean(2 * k, 2, D).then_inc(s_ms, 1)
                dve.wait_ge(s_rstd, count)
                dve.wait_ge(s_gain[k % 2], 16 * (k // 2 + 1))
                for t in range(TT):
                    dve.scalar_tensor_tensor(xn[:, t, :], h[:, t, :], rstd[:, 2 * k + t:2 * k + t + 1], gain[k % 2][:, :],
                                             ALU.mult, ALU.mult).then_inc(s_fin if k == FINAL else s_xn, 1)

            def left_lo(stage):
                for g in range(4):
                    dve.wait_ge(s_hiT, LEFT[stage] - 3 + g)
                    key = ("left", stage, g)
                    dve.tensor_tensor(xlo[:, 2 * g:2 * g + 2, :], bank(key).rearrange("p (k s) -> p k s", k=2),
                                      xhi[:, 2 * g:2 * g + 2, :].bitcast(F), ALU.subtract).then_inc(s_loT, 1)

            def add_columns(stage, c):
                for t in range(TT):
                    part = h[:, t, c * CH:(c + 1) * CH]
                    dve.tensor_tensor(part, part, bank((stage, c, t)), ALU.add).then_inc(s_res, 1)

            norm(MIX0, 1)
            upto(2)
            left_lo(0)
            dve.wait_ge(s_consts, 16)
            dve.wait_ge(s_pos, 16)
            step(dve.tensor_copy(pos_f[:], pos_i[:]))
            settle()
            for t in range(TT):
                step(dve.tensor_scalar(trig[:, 0, t, :], consts[:, C_FREQ:C_FREQ + N_FREQ], pos_f[:, t:t + 1], None, ALU.mult))
            settle()
            step(dve.tensor_scalar(trig[:, 1, :, :], trig[:, 0, :, :], 1.0 / TWO_PI, ROUND, ALU.mult, ALU.add))
            settle()
            step(dve.tensor_scalar(trig[:, 1, :, :], trig[:, 1, :, :], ROUND, None, ALU.subtract))
            settle()
            for part in TURN_PARTS:
                step(dve.scalar_tensor_tensor(trig[:, 0, :, :], trig[:, 1, :, :], -part, trig[:, 0, :, :], ALU.mult, ALU.add))
                settle()
            dve.tensor_scalar(trig[:, 0, :, :], trig[:, 0, :, :], SIN_MAX, -SIN_MAX, ALU.min, ALU.max).then_inc(s_trig, 1)
            dve.wait_ge(s_trig, 1)
            step(dve.scalar_tensor_tensor(trig[:, 1, :, :], trig[:, 0, :, :], -1.0, trig[:, 0, :, :], ALU.mult, ALU.max))
            settle()
            dve.tensor_scalar(trig[:, 1, :, :], trig[:, 1, :, :], -1.0, TWO_PI / 4, ALU.mult, ALU.add).then_inc(s_trig, 1)
            upto(3)
            dve.wait_ge(s_sq, 6)
            step(mean(LAT, 2, B_QL, 2))
            mean(LAT + 1, 2, B_KVL, 2).then_inc(s_ms, 1)
            dve.wait_ge(s_rstd, 2)
            dve.wait_ge(s_small, 48)
            for t in range(TT):
                for i, (c0, c1) in enumerate(((0, B_QL), (B_QL, B_QL + B_KVL))):
                    col = LAT + 2 * t + i
                    dve.scalar_tensor_tensor(lat[:, t, c0:c1], proj[:, t, 1536 + c0:1536 + c1], rstd[:, col:col + 1],
                                             small_g[:, c0:c1], ALU.mult, ALU.mult).then_inc(s_lat, 1)
            upto(5)
            dve.wait_ge(s_hiT, 5)
            dve.tensor_tensor(llo[:, 0:2, :], bank("lat0").rearrange("p (k s) -> p k s", k=2), lhi[:, 0:2, :].bitcast(F),
                              ALU.subtract).then_inc(s_loT, 1)
            dve.wait_ge(s_hiT, 6)
            dve.tensor_tensor(llo[:, 2, :], bank("lat1")[:, 0:S], lhi[:, 2, :].bitcast(F), ALU.subtract).then_inc(s_loT, 1)
            step(dve.tensor_scalar(g_sub, g_sub, 1.0 - LAMBDA_INIT, None, ALU.mult))
            dve.wait_ge(s_lam_in, 64)
            for i in range(2):
                last = dve.tensor_tensor_reduce(out=lam_in[:, 2 * i, :], in0=lam_in[:, 2 * i, :], in1=lam_in[:, 2 * i + 1, :],
                                                scale=1.0, scalar=0.0, op0=ALU.mult, op1=ALU.add, accum_out=lam[:, i:i + 1])
            last.then_inc(s_lam, 1)
            upto(11)
            for g in range(4):
                key = ("kB", g)
                wait_full(dve, key)
                dve.tensor_copy(kT[0:B_QK, 2 * g:2 * g + 2, :].rearrange("p k s -> p (k s)"),
                                ps[0:B_QK, use[key][0], :]).then_inc(free[use[key][0]], 1)
            upto(12)
            dve.wait_ge(s_bias, 1)

            def maxima(u):
                dve.wait_ge(s_sc, u + 1)
                if u < A_HEADS:
                    if u >= 2:
                        dve.wait_ge(s_exp, u - 1)
                    for (c0, c1) in ((0, 128), (128, 384)):
                        n = c1 - c0
                        step(dve.scalar_tensor_tensor(biased[u % 2][:, c0:c1], ps[:, 2 * (u % 2), c0:c1], A_SCALE,
                                                      bias[:, u, n - 1::-1], ALU.mult, ALU.add))
                    settle()
                maps = 1 if u < UNITS0 else 2
                for m in range(maps):
                    for t, (c0, c1) in enumerate(((0, 128), (128, 384))):
                        col = 2 * m + t
                        src = biased[u % 2][:, c0:c1] if u < A_HEADS else ps[:, 2 * (u % 2) + m, c0:c1]
                        step(dve.reduce_max(mx[:, u, col:col + 1], src, AX.X))
                settle()
                scale = 1.0 if u < A_HEADS else B_SCALE if u < UNITS0 else C_SCALE
                dve.tensor_scalar(nmx[:, u, 0:2 * maps], mx[:, u, 0:2 * maps], -scale, None, ALU.mult).then_inc(s_nm, 1)

            def head_out(u):
                step(dve.reciprocal(rden[:, u, 0:2], den[:, u, 0:2]))
                settle()
                dve.wait_ge(s_of, u + 1)
                for t in range(TT):
                    last = dve.tensor_scalar(xn[:, t, 64 * u:64 * u + 64], ps[:, 6 + u % 2, 64 * t:64 * t + 64],
                                             rden[:, u, t:t + 1], None, ALU.mult)
                last.then_inc(s_mix, 1)

            maxima(0)
            maxima(1)
            for u in range(UNITS0):
                if u + 2 < UNITS0:
                    maxima(u + 2)
                head_out(u)
            left_lo(1)
            upto(13)
            dve.wait_ge(s_used, T_OUT0 + 2)
            add_columns("out0", 0)
            upto(15)
            dve.wait_ge(s_used, T_OUT0 + 4)
            add_columns("out0", 1)
            norm(FFN0, 3)
            left_lo(2)
            upto(T_FFN + 5)

            def hidden(j, width=CH):
                dve.wait_ge(f_act, j + 1)
                dve.tensor_tensor(hid[:, :, 0:width], act_g[:, :, 0:width], ps[:, 2:4, 0:width], ALU.mult).then_inc(f_h, 1)

            def hid_lo(j, k=4):
                dve.wait_ge(f_hhi, j + 1)
                dve.tensor_tensor(hidlo[:, 0:k, :], ps[:, 4:6, :].rearrange("p b (k s) -> p (b k) s", k=2)[:, 0:k, :],
                                  hidhi[:, 0:k, :].bitcast(F), ALU.subtract).then_inc(f_ht, 1)

            def add_down(t, half):
                part = h[:, t, half * CH:(half + 1) * CH]
                dve.tensor_tensor(part, part, ps[:, 6 + t, :], ALU.add).then_inc(f_add, 1)

            dve.wait_ge(s_used, T_FFN + 4)
            hidden(0)
            with dve.Fori(1, N_FULL) as j:
                def split_next(r):
                    n = T_FFN + 4 + r
                    dve.wait_ge(s_hi, (j - 1) * 6 + (n + 1))
                    dve.tensor_tensor(wlo[n % SPLIT][:, :], raw[n % RAW][:, :], whi[n % SPLIT][:, :].bitcast(F),
                                      ALU.subtract).then_inc(s_lo, 1)

                split_next(2)
                split_next(3)
                hid_lo(j - 1)
                split_next(4)
                split_next(5)
                dve.wait_ge(s_used, (j - 1) * 6 + (T_FFN + 8))
                hidden(j)
                split_next(6)
                dve.wait_ge(f_d, j * 2 - 1)
                add_down(0, 0)
                dve.wait_ge(s_used, (j - 1) * 6 + (T_FFN + 9))
                add_down(1, 0)
                split_next(7)
                dve.wait_ge(f_d, j * 2)
                add_down(0, 1)
                dve.wait_ge(s_used, (j - 1) * 6 + (T_FFN + 10))
                add_down(1, 1)
            done[0] = T_LAST + 2
            upto(T_LAST + 2)
            hid_lo(LAST - 1)
            upto(T_LAST + 3)
            dve.wait_ge(s_used, T_LAST + 2)
            hidden(LAST, 256)
            for half in range(2):
                upto(T_LAST + 4 + half)
                dve.wait_ge(f_d, 2 * LAST - 1 + half)
                add_down(0, half)
                dve.wait_ge(s_used, T_LAST + 3 + half)
                add_down(1, half)
            hid_lo(LAST, 2)
            upto(T_LAST + 6)
            for i in range(4):
                if i < 3:
                    dve.wait_ge(f_d, 2 * LAST + 1 + i)
                else:
                    dve.wait_ge(s_used, T_LAST + 5)
                add_down(i % 2, i // 2)
            norm(MIX1, 4)
            left_lo(3)

            dve.wait_ge(s_pool, 4)
            for c in range(4):
                upto(T_IN1 + 2 * c + 3)
                dve.wait_ge(s_used, T_IN1 + 2 * c + 2)
                for t in range(TT):
                    key = ("in1", c, t)
                    x = bank(key).rearrange("p (a b) -> p a b", a=8)
                    r0, r1 = [r[:, :].rearrange("p (a b) -> p a b", a=8) for r in rot]
                    step(dve.tensor_tensor(r0, x, spread(cc[:, t, :], [P, 8, C_DH], 1), ALU.mult))
                    step(dve.tensor_tensor(r1[:, :, 0:32], x[:, :, 32:64], spread(ss[:, t, 0:32], [P, 8, 32], 1), ALU.mult))
                    dve.tensor_tensor(r1[:, :, 32:64], x[:, :, 0:32], spread(ss[:, t, 32:64], [P, 8, 32], 1),
                                      ALU.mult).then_inc(free[use[key][0]], 1)
                    settle()
                    wait_free(dve, key)
                    dve.tensor_tensor(proj1[:, t, c * CH:(c + 1) * CH], rot[0][:, :], rot[1][:, :], ALU.add).then_inc(s_rot, 1)
                    dve.wait_ge(s_rot, 2 * c + t + 1)
                if c == 1:
                    dve.wait_ge(s_wr, 1)
                    dve.tensor_tensor(wrlo[:], wr[:], wrhi[:].bitcast(F), ALU.subtract).then_inc(s_wr, 1)
            dve.wait_ge(s_lam, 2)
            step(dve.tensor_tensor(lam[:, 4:5], lam[:, 2:3], lam[:, 3:4], ALU.subtract))
            settle()
            step(dve.tensor_scalar(lam[:, 5:6], lam[:, 4:5], LAMBDA_INIT, None, ALU.add))
            upto(T_OUT1 + 2)

            def difference(u):
                dve.wait_ge(s_exp, u + 1)
                step(dve.reciprocal(rden[:, u, :], den[:, u, :]))
                settle()
                step(dve.tensor_scalar(rden[:, u, 2:4], rden[:, u, 2:4], lam[:, 5:6], None, ALU.mult))
                settle()
                if u >= UNITS0 + 2:
                    dve.wait_ge(s_ptf, u - 1)
                for t, (c0, c1) in enumerate(((0, 128), (128, 384))):
                    step(dve.tensor_scalar(scaled2[:, c0:c1], probs1[u % 2][:, 1, c0:c1], rden[:, u, 2 + t:3 + t], None, ALU.mult))
                settle()
                for t, (c0, c1) in enumerate(((0, 128), (128, 384))):
                    last = dve.scalar_tensor_tensor(diff[u % 2][:, c0:c1], probs1[u % 2][:, 0, c0:c1], rden[:, u, t:t + 1],
                                                    scaled2[:, c0:c1], ALU.mult, ALU.subtract)
                last.then_inc(s_diff, 1)
                dve.wait_ge(s_diff, u - UNITS0 + 1)

            maxima(UNITS0)
            maxima(UNITS0 + 1)
            for u in range(UNITS0, UNITS):
                difference(u)
                if u + 2 < UNITS:
                    maxima(u + 2)
                dve.wait_ge(s_of, u + 1)
                hd = u - UNITS0
                dve.tensor_copy(xn[:, :, hd * C_DV:(hd + 1) * C_DV],
                                ps[:, 6 + u % 2, 0:2 * C_DV].rearrange("p (t d) -> p t d", t=TT)).then_inc(s_mix, 1)
            dve.wait_ge(s_sqc, C_HEADS)
            mean(SUBLN, 16, C_DV).then_inc(s_ms, 1)
            dve.wait_ge(s_rstd, 5)
            for t in range(TT):
                heads = xn[:, t, :].rearrange("p (a b) -> p a b", a=C_HEADS)
                scale = spread(rstd[:, SUBLN + 8 * t:SUBLN + 8 * t + 8], [P, C_HEADS, C_DV], 2)
                step(dve.tensor_tensor(heads, heads, scale, ALU.mult))
                settle()
                dve.tensor_tensor(heads, heads, spread(g_sub, [P, C_HEADS, C_DV], 1), ALU.mult).then_inc(s_sub, 1)
            left_lo(4)
            upto(T_OUT1 + 3)
            dve.wait_ge(s_used, T_OUT1 + 2)
            add_columns("out1", 0)
            dve.wait_ge(s_used, T_OUT1 + 4)
            add_columns("out1", 1)
            norm(FFN1, 6)
            for t in range(TT):
                dve.wait_ge(s_tok, t + 1)
                dve.tensor_tensor(tlo[:, t, :], xn[:, t, :], thi[:, t, :].bitcast(F), ALU.subtract).then_inc(s_tlo, 1)
            left_lo(5)

            def grid(x):
                return spread(x, [P, TT, 8], 2)

            def over_tiles(x):
                return spread(x, [P, TT, 8], 1)

            dve.wait_ge(s_log, 1)
            step(dve.tensor_copy(logit[:], ps[:, 0, 0:16].rearrange("p (t e) -> p t e", t=TT)))
            settle()
            src = logit
            for i in range(2):
                step(dve.reduce_max(rs[:, 2 * i, :], src[:] if i == 0 else rt[:, 0, :, :], AX.X))
                settle()
                step(dve.tensor_tensor(rt[:, 1, :, :], src[:] if i == 0 else rt[:, 0, :, :], grid(rs[:, 2 * i, :]), ALU.is_equal))
                settle()
                step(dve.tensor_tensor(rt[:, 1, :, :], rt[:, 1, :, :], over_tiles(r8), ALU.mult))
                settle()
                step(dve.reduce_max(rs[:, 2 * i + 1, :], rt[:, 1, :, :], AX.X))
                settle()
                step(dve.tensor_tensor(rt[:, 2 + i, :, :], rt[:, 1, :, :], grid(rs[:, 2 * i + 1, :]), ALU.is_equal))
                settle()
                if i == 0:
                    step(dve.scalar_tensor_tensor(rt[:, 0, :, :], rt[:, 2, :, :], -3.0e38, logit[:], ALU.mult, ALU.add))
                    settle()
            dve.tensor_tensor(rs[:, 4, :], rs[:, 2, :], rs[:, 0, :], ALU.subtract).then_inc(s_dlt, 1)
            dve.tensor_tensor(chosen[:, :, 0:8], rt[:, 2, :, :], rt[:, 3, :, :], ALU.add).then_inc(s_cho, 1)
            dve.wait_ge(s_ex, 1)
            step(dve.tensor_scalar(rs[:, 6, :], rs[:, 5, :], 1.0, None, ALU.add))
            settle()
            step(dve.reciprocal(rs[:, 7, :], rs[:, 6, :]))
            settle()
            step(dve.tensor_tensor(rs[:, 8, :], rs[:, 5, :], rs[:, 7, :], ALU.mult))
            settle()
            step(dve.tensor_tensor(rt[:, 4, :, :], rt[:, 2, :, :], grid(rs[:, 7, :]), ALU.mult))
            step(dve.tensor_tensor(rt[:, 5, :, :], rt[:, 3, :, :], grid(rs[:, 8, :]), ALU.mult))
            settle()
            step(dve.tensor_tensor(gate[:, :, 0:8], rt[:, 4, :, :], rt[:, 5, :, :], ALU.add))
            step(dve.memset(scan[:], 0.0))
            dve.wait_ge(s_rank, 1)
            step(dve.tensor_copy(slot[:, :, 0:8], ps[:, 1, 0:16].rearrange("p (t e) -> p t e", t=TT)))
            settle()
            step(dve.tensor_scalar(scan[:, 0, 8:16], ps[:, 1, 16:24], float(P), None, ALU.is_gt))
            settle()
            for i, shift in enumerate((1, 2, 4)):
                step(dve.tensor_tensor(scan[:, i + 1, 8:16], scan[:, i, 8:16], scan[:, i, 8 - shift:16 - shift], ALU.add))
                settle()
            step(dve.tensor_copy(order[:, 0:8], e8))
            step(dve.memset(order[:, 11:15], 0.0))
            step(dve.tensor_scalar(order[:, 15:16], scan[:, 3, 15:16], float(N_EXP), None, ALU.add))
            for q in range(MAX_PASS - N_EXP):
                step(dve.scalar_tensor_tensor(rt[:, 6, 0, :], scan[:, 3, 8:16], q + 1.0, scan[:, 0, 8:16], ALU.is_equal, ALU.mult))
                settle()
                step(dve.tensor_tensor(rt[:, 6, 1, :], rt[:, 6, 0, :], e8, ALU.mult))
                for i, table in enumerate((chosen, slot, gate)):
                    step(dve.tensor_tensor(rt[:, 7 + i, :, :], table[:, :, 0:8], over_tiles(rt[:, 6, 0, :]), ALU.mult))
                settle()
                step(dve.reduce_sum(order[:, 8 + q:9 + q], rt[:, 6, 1, :], AX.X))
                step(dve.reduce_sum(chosen[:, :, 8 + q], rt[:, 7, :, :], AX.X))
                step(dve.reduce_sum(rs[:, 9, :], rt[:, 8, :, :], AX.X))
                step(dve.reduce_sum(gate[:, :, 8 + q], rt[:, 9, :, :], AX.X))
                settle()
                step(dve.tensor_scalar(slot[:, :, 8 + q], rs[:, 9, :], -float(P), None, ALU.add))
            settle()
            dve.tensor_copy(order_i[:], order[:]).then_inc(s_order, 1)
            dve.wait_ge(s_order, 1)

            passes = dve.value_load(order_i[0:1, 15:16], min_val=N_EXP, max_val=MAX_PASS)
            with dve.Fori(0, passes) as p:
                def split_tile(i, turns=0):
                    n = T_MOE + i
                    dve.wait_ge(s_hi, p * M_TILES + turns * 6 + (n + 1))
                    dve.tensor_tensor(wlo[n % SPLIT][:, :], raw[n % RAW][:, :], whi[n % SPLIT][:, :].bitcast(F),
                                      ALU.subtract).then_inc(s_lo, 1)

                def hidden_e(j):
                    dve.wait_ge(m_act, p * M_CH + j + 1)
                    dve.tensor_tensor(hid_e[:], act_e[:], ps[:, 1, :], ALU.mult).then_inc(m_h, 1)

                def hid_lo_e(j):
                    dve.wait_ge(m_thi, p * M_CH + j + 1)
                    dve.tensor_tensor(helo[:], ps[:, 2, :].rearrange("p (k s) -> p k s", k=4), hehi[:].bitcast(F),
                                      ALU.subtract).then_inc(m_tr, 1)

                dve.tensor_copy(gcur[:], gate[:, :, ds(p, 1)].rearrange("p t o -> p (t o)"))
                for t in range(TT):
                    last = dve.tensor_scalar(sel[:, t, :], iota, slot[:, t, ds(p, 1)], chosen[:, t, ds(p, 1)],
                                             ALU.is_equal, ALU.mult)
                last.then_inc(m_sel, 1)
                for i in range(3):
                    split_tile(i)
                dve.wait_ge(m_xhi, p + 1)
                dve.tensor_tensor(xglo[:], ps[:, 6:8, :].rearrange("p b (k s) -> p (b k) s", k=4), xghi[:].bitcast(F),
                                  ALU.subtract).then_inc(m_xlo, 1)
                dve.wait_ge(m_aux, p + 1)
                dve.tensor_copy(selT[:], ps[:, 5, 0:S])
                dve.tensor_copy(gslot[:], ps[:, 5, S:S + 1]).then_inc(m_auxr, 1)
                for i in range(3, 6):
                    split_tile(i)
                dve.wait_ge(s_used, p * M_TILES + (T_MOE + 4))
                hidden_e(0)
                with dve.Fori(1, M_CH) as j:
                    split_tile(6, j - 1)
                    split_tile(7, j - 1)
                    hid_lo_e(j - 1)
                    split_tile(8, j - 1)
                    split_tile(9, j - 1)
                    dve.wait_ge(s_used, p * M_TILES + j * 6 + (T_MOE + 2))
                    hidden_e(j)
                    split_tile(10, j - 1)
                    split_tile(11, j - 1)
                hid_lo_e(M_CH - 1)
                dve.wait_ge(m_yhi, p + 1)
                dve.wait_ge(m_auxr, p + 1)
                dve.scalar_tensor_tensor(ylo[:], ps[:, 3:5, :].rearrange("p b n -> p (b n)"), gslot[:, 0:1],
                                         yhi[:].bitcast(F), ALU.mult, ALU.subtract).then_inc(m_ylo, 1)
                for i in range(4):
                    dve.wait_ge(m_acc, p * 4 + i + 1)
                    part = h[:, i // 2, (i % 2) * CH:(i % 2 + 1) * CH]
                    dve.tensor_tensor(part, part, ps[:, 6 + i % 2, :], ALU.add).then_inc(m_add, 1)
            norm(FINAL, 7)

        @block.tensor
        def _(pe):
            def three(out, left, right, cols, start, stop):
                for i, (l, r) in enumerate(((0, 0), (0, 1), (1, 0))):
                    last = pe.matmul(out, left[l], right[r], start=start and i == 0, stop=stop and i == 2)
                return last

            def tile(n, k, m):
                return [w[n % SPLIT][:, 0:k * m].rearrange("p (k m) -> p k m", k=k) for w in (whi, wlo)]

            def acquire(key):
                if use[key][2]:
                    pe.wait_ge(free[use[key][0]], use[key][2])

            def all_read(counts):
                for b, n in enumerate(counts):
                    if n:
                        pe.wait_ge(free[b], n)

            def transposes(key, blocks):
                acquire(key)
                for i, src in enumerate(blocks):
                    m = src.shape[1]
                    last = pe.transpose(ps[0:m, use[key][0], i * P:(i + 1) * P], src, ident)
                last.then_inc(full[use[key][0]], 1)

            def left_operand(stage, src):
                for g in range(4):
                    prior = LEFT[stage] - 4 + g - 2
                    if g >= 2:
                        pe.wait_ge(s_loT, prior + 1)
                    key = ("left", stage, g)
                    for i, (k, t) in enumerate(((2 * g, 0), (2 * g, 1), (2 * g + 1, 0), (2 * g + 1, 1))):
                        last = pe.transpose(ps[:, use[key][0], i * P:(i + 1) * P], src[:, t, k * P:(k + 1) * P], ident)
                    last.then_inc(full[use[key][0]], 1)

            def columns(stage, c, n, width=CH, blocks=KB):
                for t in range(TT):
                    acquire((stage, c, t))
                for b in range(2):
                    pe.wait_ge(s_lo, n + b + 1)
                    w = tile(n + b, 4, width)
                    for t in range(TT):
                        for k in range(4):
                            kb = 4 * b + k
                            last = three(bank((stage, c, t))[:, 0:width],
                                         [x[:, kb, t * P:(t + 1) * P] for x in (xhi, xlo)],
                                         [x[:, k, :] for x in w], width, kb == 0, kb == KB - 1)
                    last.then_inc(s_used, 1)

            pe.wait_ge(s_consts, 16)
            pe.wait_ge(s_xn, 2)
            left_operand(0, xn)
            pe.wait_ge(s_loT, LEFT[0])
            columns("in0", 3, T_IN0, 416)
            columns("in0", 0, T_IN0 + 2)
            pe.wait_ge(s_lat, 4)
            transposes("lat0", [lat[:, t, k * P:(k + 1) * P] for k in range(2) for t in range(TT)])
            transposes("lat1", [lat[:, t, B_QL:B_QL + B_KVL] for t in range(TT)])
            columns("in0", 1, T_IN0 + 4)
            pe.wait_ge(s_loT, 6)
            pe.wait_ge(s_lo, T_UQ + 1)
            w = tile(T_UQ, 2, 768)
            for c, width in ((0, CH), (1, 768 - CH)):
                for t in range(TT):
                    acquire(("uq", c, t))
                    for k in range(2):
                        last = three(bank(("uq", c, t))[:, 0:width], [x[:, k, t * P:(t + 1) * P] for x in (lhi, llo)],
                                     [x[:, k, c * CH:c * CH + width] for x in w], width, k == 0, k == 1)
            last.then_inc(s_used, 1)
            pe.wait_ge(s_lo, T_UKV + 1)
            w = tile(T_UKV, 1, D)
            for c in range(2):
                for t in range(TT):
                    acquire(("ukv", c, t))
                    last = three(bank(("ukv", c, t)), [x[:, 2, t * P:(t + 1) * P] for x in (lhi, llo)],
                                 [x[:, 0, c * CH:(c + 1) * CH] for x in w], CH, True, True)
            last.then_inc(s_used, 1)
            for name, c in (("qA", 0), ("kA", 1)):
                for t in range(TT):
                    wait_free(pe, ("in0", c, t))
                for g in range(2):
                    transposes((name, g), [proj[:, t, c * CH + k * P:c * CH + (k + 1) * P]
                                           for k in (2 * g, 2 * g + 1) for t in range(TT)])
            columns("in0", 2, T_IN0V)
            pe.wait_ge(s_rope, 8)
            for t in range(TT):
                for c in range(2):
                    wait_free(pe, ("ukv", c, t))
            for name, src in (("qB", qB), ("kB", kB)):
                for g in range(4):
                    transposes((name, g), [src[:, t, hd, :] for hd in (2 * g, 2 * g + 1) for t in range(TT)])

            def scores(u):
                if u >= 2:
                    pe.wait_ge(s_exp, u - 1)
                for m in range(1 if u < UNITS0 else 2):
                    if u < A_HEADS:
                        rows = slice(64 * (u % 2), 64 * (u % 2) + 64)
                        q, k = qTA[rows, u // 2, :], kTA[rows, u // 2, :]
                    elif u < UNITS0:
                        q, k = qT[0:B_QK, u - A_HEADS, :], kT[0:B_QK, u - A_HEADS, :]
                    else:
                        rows = slice(64 * m, 64 * m + 64)
                        q, k = qTC[rows, u - UNITS0, :], kTC[rows, u - UNITS0, :]
                    b = 2 * (u % 2) + m
                    masked = u >= A_HEADS
                    for t in range(TT):
                        c0, c1 = ((0, 128), (128, 384))[t]
                        last = pe.matmul(ps[:, b, c0:c1], q[:, t * P:(t + 1) * P], k[:, 0:c1 - c0], start=True, stop=not masked)
                        if masked:
                            last = pe.matmul(ps[:, b, c1 - 64:c1], ident, mask, start=False, stop=True)
                last.then_inc(s_sc, 1)

            def unit(u, src, value, width, ready, count, last_unit):
                pe.wait_ge(ready, count)
                if u >= 2:
                    pe.wait_ge(s_pT, u - 1)
                for i in range(3):
                    last = pe.transpose(ps[:, 4 + u % 2, i * P:(i + 1) * P], src[:, i * P:(i + 1) * P], ident)
                last.then_inc(s_ptf, 1)
                if u + 2 < last_unit:
                    scores(u + 2)
                pe.wait_ge(s_pT, u + 1)
                if u >= 2:
                    pe.wait_ge(s_mix, u - 1)
                out = ps[:, 6 + u % 2, :]
                dst = probsT if u < UNITS0 else diffT
                pe.matmul(out[:, 0:width], dst[u % 2][:, 0:P], value(0), start=True, stop=True)
                pe.matmul(out[:, width:2 * width], dst[u % 2][:, P:2 * P], value(0), start=True, stop=False)
                pe.matmul(out[:, width:2 * width], dst[u % 2][:, 2 * P:3 * P], value(1), start=False, stop=True)\
                    .then_inc(s_of, 1)

            all_read(before_units0)
            scores(0)
            scores(1)
            for u in range(UNITS0):
                def value(t):
                    return proj[:, t, 1024 + 64 * u:1088 + 64 * u] if u < A_HEADS else vB[:, t, u - A_HEADS, :]
                unit(u, probs[u % 2], value, 64, s_exp, u + 1, UNITS0)
            pe.wait_ge(s_mix, UNITS0)
            left_operand(1, xn)
            pe.wait_ge(s_loT, LEFT[1])
            for c in range(2):
                columns("out0", c, T_OUT0 + 2 * c)
            pe.wait_ge(s_xn, 4)
            left_operand(2, xn)
            pe.wait_ge(s_loT, LEFT[2])

            def dense(n, b, first, width=CH, kb=4):
                w = tile(n, kb, width)
                for t in range(TT):
                    for k in range(kb):
                        last = three(ps[:, b + t, 0:width], [x[:, first + k, t * P:(t + 1) * P] for x in (xhi, xlo)],
                                     [x[:, k, :] for x in w], width, first + k == 0, first + k == KB - 1)
                last.then_inc(s_used, 1)

            def hid_transposes(j, k=4):
                pe.wait_ge(f_h, j + 1)
                for i in range(k):
                    for t in range(TT):
                        at = (2 * (i % 2) + t) * P
                        last = pe.transpose(ps[:, 4 + i // 2, at:at + P], hid[:, t, i * P:(i + 1) * P], ident)
                last.then_inc(f_t, 1)

            for r in range(4):
                pe.wait_ge(s_lo, T_FFN + r + 1)
                dense(T_FFN + r, 2 * (r // 2), 4 * (r % 2))
            with pe.Fori(1, N_FULL) as j:
                for r in range(6):
                    n = T_FFN + 4 + r
                    if r == 0:
                        pe.wait_ge(f_act, j * 1)
                    if r == 2:
                        hid_transposes(j - 1)
                    if r == 4:
                        pe.wait_ge(f_ht, j * 1)
                    pe.wait_ge(s_lo, (j - 1) * 6 + (n + 1))
                    if r < 4:
                        dense(n, 2 * (r // 2), 4 * (r % 2))
                    else:
                        w = tile(n, 4, CH)
                        for t in range(TT):
                            if r == 5:
                                pe.wait_ge(f_add, (j - 1) * 4 + 1 + t)
                            for k in range(4):
                                last = three(ps[:, 6 + t, :], [x[:, k, t * P:(t + 1) * P] for x in (hidhi, hidlo)],
                                             [x[:, k, :] for x in w], CH, k == 0, k == 3)
                            last.then_inc(f_d if t == 0 else s_used, 1)
            pe.wait_ge(f_act, LAST)
            pe.wait_ge(s_lo, T_LAST + 1)
            dense(T_LAST, 0, 0, 256, KB)
            hid_transposes(LAST - 1)
            pe.wait_ge(s_lo, T_LAST + 2)
            dense(T_LAST + 1, 2, 0, 256, KB)
            pe.wait_ge(f_ht, LAST)
            for half in range(2):
                n = T_LAST + 2 + half
                pe.wait_ge(s_lo, n + 1)
                w = tile(n, 4, CH)
                for t in range(TT):
                    pe.wait_ge(f_add, 4 * (LAST - 1) + (1 + t if half else 0))
                    for k in range(4):
                        last = three(ps[:, 6 + t, :], [x[:, k, t * P:(t + 1) * P] for x in (hidhi, hidlo)],
                                     [x[:, k, :] for x in w], CH, k == 0, k == 3)
                    last.then_inc(f_d if t == 0 else s_used, 1)
            hid_transposes(LAST, 2)
            pe.wait_ge(f_ht, LAST + 1)
            pe.wait_ge(s_lo, T_LAST + 5)
            w = tile(T_LAST + 4, 2, D)
            for i in range(4):
                half, t = i // 2, i % 2
                pe.wait_ge(f_add, 4 * LAST + i - 1)
                for k in range(2):
                    last = three(ps[:, 6 + t, :], [x[:, k, t * P:(t + 1) * P] for x in (hidhi, hidlo)],
                                 [x[:, k, half * CH:(half + 1) * CH] for x in w], CH, k == 0, k == 1)
                last.then_inc(f_d if i < 3 else s_used, 1)

            pe.wait_ge(s_xn, 6)
            left_operand(3, xn)
            pe.wait_ge(s_loT, LEFT[3])
            for c in range(6):
                columns("in1", c, T_IN1 + 2 * c)
                if c in (2, 4):
                    name, c0 = ("qC", 0) if c == 2 else ("kC", 2)
                    pe.wait_ge(s_rot, 2 * c0 + 4)
                    for g in range(4):
                        transposes((name, g), [proj1[:, t, c0 * CH + k * P:c0 * CH + (k + 1) * P]
                                               for k in (2 * g, 2 * g + 1) for t in range(TT)])
            all_read(before_units1)
            scores(UNITS0)
            scores(UNITS0 + 1)
            for u in range(UNITS0, UNITS):
                def value(t):
                    at = 2 * D + C_DV * (u - UNITS0)
                    return proj1[:, t, at:at + C_DV]
                unit(u, diff[u % 2], value, C_DV, s_diff, u - UNITS0 + 1, UNITS)
            pe.wait_ge(s_sub, TT)
            left_operand(4, xn)
            pe.wait_ge(s_loT, LEFT[4])
            for c in range(2):
                columns("out1", c, T_OUT1 + 2 * c)
            pe.wait_ge(s_xn, 8)
            left_operand(5, xn)
            pe.wait_ge(s_loT, LEFT[5])
            pe.wait_ge(s_wr, 2)
            for t in range(TT):
                for k in range(KB):
                    last = three(ps[:, 0, 8 * t:8 * t + 8], [x[:, k, t * P:(t + 1) * P] for x in (xhi, xlo)],
                                 [wrhi[:, k, :], wrlo[:, k, :]], 8, k == 0, k == KB - 1)
            last.then_inc(s_log, 1)
            pe.wait_ge(s_cho, 1)
            pe.matmul(ps[:, 1, 0:8], tri, chosen[:, 0, 0:8], start=True, stop=True)
            pe.matmul(ps[:, 1, 8:16], ones, chosen[:, 0, 0:8], start=True, stop=False)
            pe.matmul(ps[:, 1, 8:16], tri, chosen[:, 1, 0:8], start=False, stop=True)
            pe.matmul(ps[:, 1, 16:24], ones, chosen[:, 0, 0:8], start=True, stop=False)
            pe.matmul(ps[:, 1, 16:24], ones, chosen[:, 1, 0:8], start=False, stop=True).then_inc(s_rank, 1)

            pe.wait_ge(s_order, 1)
            pe.wait_ge(s_tlo, TT)
            passes = pe.value_load(order_i[0:1, 15:16], min_val=N_EXP, max_val=MAX_PASS)
            with pe.Fori(0, passes) as p:
                def ready(i, turns=0):
                    pe.wait_ge(s_lo, p * M_TILES + turns * 6 + (T_MOE + i + 1))

                def expert(i, b, first):
                    w = tile(T_MOE + i, 4, CH)
                    for k in range(4):
                        last = three(ps[:, b, :], [xghi[:, first + k, :], xglo[:, first + k, :]],
                                     [x[:, k, :] for x in w], CH, first + k == 0, first + k == KB - 1)
                    last.then_inc(s_used, 1)

                def hid_transposes_e(j):
                    pe.wait_ge(m_h, p * M_CH + j + 1)
                    for i in range(4):
                        last = pe.transpose(ps[:, 2, i * P:(i + 1) * P], hid_e[:, i * P:(i + 1) * P], ident)
                    last.then_inc(m_t, 1)

                def down_e(i, half, start, stop):
                    w = tile(T_MOE + i, 4, CH)
                    for k in range(4):
                        last = three(ps[:, 3 + half, :], [hehi[:, k, :], helo[:, k, :]], [x[:, k, :] for x in w],
                                     CH, start and k == 0, stop and k == 3)
                    last.then_inc(s_used, 1)

                pe.wait_ge(m_sel, p + 1)
                for k in range(KB):
                    for t in range(TT):
                        for i, x in enumerate((thi, tlo)):
                            last = pe.matmul(ps[:, 6 + k // 4, (k % 4) * P:(k % 4 + 1) * P], x[:, t, k * P:(k + 1) * P],
                                             sel[:, t, :], start=t == 0 and i == 0, stop=t == 1 and i == 1)
                last.then_inc(m_x, 1)
                for t in range(TT):
                    pe.transpose(ps[:, 5, t * P:(t + 1) * P], sel[:, t, :].bitcast(F), ident)
                for t in range(TT):
                    last = pe.matmul(ps[:, 5, S:S + 1], sel[:, t, :].bitcast(F), gcur[:, t:t + 1], start=t == 0, stop=t == 1)
                last.then_inc(m_aux, 1)
                pe.wait_ge(m_xlo, p + 1)
                for i in range(4):
                    ready(i)
                    expert(i, i // 2, 4 * (i % 2))
                def turn(j, start, turns):
                    for r in range(6):
                        if r == 2:
                            hid_transposes_e(j - 1)
                        if r == 0:
                            pe.wait_ge(m_act, p * M_CH + j)
                        if r == 4:
                            pe.wait_ge(m_tr, p * M_CH + j)
                        ready(4 + r, turns)
                        if r < 4:
                            expert(4 + r, r // 2, 4 * (r % 2))
                        else:
                            down_e(4 + r, r - 4, start, False)

                turn(1, True, 0)
                with pe.Fori(2, M_CH) as j:
                    turn(j, False, j - 1)
                hid_transposes_e(M_CH - 1)
                pe.wait_ge(m_tr, p * M_CH + M_CH)
                for half in range(2):
                    ready(M_TILES - 2 + half)
                    down_e(M_TILES - 2 + half, half, False, True)
                pe.wait_ge(m_ylo, p + 1)
                for i in range(4):
                    t, half = i // 2, i % 2
                    if i >= 2:
                        pe.wait_ge(m_add, p * 4 + (i - 1))
                    for n, y in enumerate((yhi, ylo)):
                        last = pe.matmul(ps[:, 6 + half, :], selT[:, t * P:(t + 1) * P], y[:, half * CH:(half + 1) * CH],
                                         start=n == 0, stop=n == 1)
                    last.then_inc(m_acc, 1)


_INS = ["x", "positions", "mix_norm_g", "ffn_norm_g", "w_in_even", "rel_bias_a", "q_norm_b", "w_uq_b", "kv_norm_b",
        "w_ukv_b", "w_out_even", "w_in_odd", "lambda_q1", "lambda_k1", "lambda_q2", "lambda_k2", "subln_g",
        "w_out_odd", "w_gu_dense", "w_down_dense", "w_router", "w_gu_moe", "w_down_moe", "final_norm_g"]


def constants():
    c = np.zeros((P, C_COLS), np.float32)
    c[:, C_ID:C_ID + P] = np.eye(P)
    c[:, C_TRI:C_TRI + P] = np.triu(np.ones((P, P)), 1)
    c[:, C_ONES:C_ONES + P] = 1.0
    c[:, C_IOTA:C_IOTA + P] = np.arange(P)
    c[0:64, C_MASK:C_MASK + 64] = NEG
    at = C_FREQ
    for dim in (B_ROPE, C_DH):
        power = np.power(np.float32(10000.0), np.arange(0, dim, 2, dtype=np.float32) / np.float32(dim))
        c[:, at:at + dim // 2] = np.float32(1.0) / power
        at += dim // 2
    c[:, C_E8:C_E8 + 8] = np.arange(8)
    c[:, C_R8:C_R8 + 8] = 8 - np.arange(8)
    return c


def kernel(**inputs):
    import concourse.bacc as bacc
    from concourse.bass_utils import run_bass_kernel_spmd

    nc = bacc.Bacc("TRN2", target_bir_lowering=False, num_devices=1)
    arrays, aps = {}, {}
    for name in _INS:
        arrays[name] = np.ascontiguousarray(inputs[name])
    arrays["consts"] = constants()
    for name, v in arrays.items():
        aps[name] = nc.dram_tensor(name, v.shape, mybir.dt.from_np(v.dtype), kind="ExternalInput").ap()
    aps["out"] = nc.dram_tensor("out", (1, S, D), mybir.dt.float32, kind="ExternalOutput").ap()
    build(nc, aps)
    r = run_bass_kernel_spmd(nc, [arrays], core_ids=[0])
    return r.results[0]["out"]
```

```python
import concourse.bass as bass
from concourse import mybir
from contextlib import ExitStack
import numpy as np

P = 128
D = 1024
S = 256
TT = S // P
KB = D // P
EVEN_IN = 1952
A_HEADS, A_DH = 8, 64
B_HEADS, B_NOPE, B_ROPE, B_V = 8, 64, 32, 64
B_QK = B_NOPE + B_ROPE
B_QL, B_KVL = 256, 128
C_HEADS, C_DH, C_DV = 8, 64, 128
FF_DENSE = 2816
N_EXP, FF_EXP = 8, 3584
EPS = 1e-6
NEG = -1.0e30
A_SCALE = A_DH ** -0.5
B_SCALE = B_QK ** -0.5
C_SCALE = C_DH ** -0.5
LAMBDA_INIT = 0.8 - 0.6 * float(np.exp(-0.3))
CH = 512
MAX_PASS = N_EXP + 3

C_ID, C_TRI, C_ONES, C_IOTA = 0, 128, 256, 384
C_MASK, C_FREQ, C_E8, C_R8, C_FOLD = 512, 576, 624, 632, 640
C_COLS = 648


WARM_FIRST, WARM_PROBS, WARM_T = 8, (0, 1), 3
N_FREQ = 48

RAW, SPLIT = 6, 3
T_IN0, T_UQ, T_UKV, T_IN0V, T_OUT0 = 0, 6, 7, 8, 10
T_FFN = 14
N_FULL = FF_DENSE // CH
T_IN1 = T_FFN + 6 * N_FULL + 3
T_OUT1 = T_IN1 + 12
T_MOE = T_OUT1 + 4
M_CH = FF_EXP // CH
M_TILES = 6 * M_CH
IN0_ORDER = [3, 0, 1, 2]
TWO_PI = 2 * float(np.pi)
TURN_PARTS = (6.28125, 0.0019340515136718750, TWO_PI - 6.28125 - 0.0019340515136718750)
ROUND = 1.5 * 2.0 ** 23
SIN_MAX = 3.1415925


def build(nc, a):
    F, R, I32 = mybir.dt.float32, mybir.dt.float32r, mybir.dt.int32
    ALU, ACT, AX = mybir.AluOpType, mybir.ActivationFunctionType, mybir.AxisListType
    ds = bass.ds

    w_in0 = a["w_in_even"][0].rearrange("(k p) n -> p k n", p=P)
    w_uq = a["w_uq_b"][0].rearrange("(k p) n -> p k n", p=P)
    w_ukv = a["w_ukv_b"][0]
    w_out0 = a["w_out_even"][0].rearrange("(k p) n -> p k n", p=P)
    w_gu = a["w_gu_dense"][0].rearrange("(k p) n -> p k n", p=P)
    w_dn = a["w_down_dense"][0].rearrange("(k p) n -> p k n", p=P)
    w_in1 = a["w_in_odd"][0].rearrange("(k p) n -> p k n", p=P)
    w_out1 = a["w_out_odd"][0].rearrange("(k p) n -> p k n", p=P)
    e_gu = a["w_gu_moe"][0].rearrange("e (k p) n -> e p k n", p=P)
    e_dn = a["w_down_moe"][0].rearrange("e (k p) n -> e p k n", p=P)

    ctx = ExitStack()
    with ctx:
        def sb(name, shape, dt=F, where=ctx):
            return where.enter_context(nc.sbuf_tensor(name, shape, dt))

        def sem(name):
            return ctx.enter_context(nc.semaphore(name))

        raw = [sb(f"raw{i}", [P, 2048]) for i in range(RAW)]
        whi = [sb(f"whi{i}", [P, 2048], R) for i in range(SPLIT)]
        wlo = [sb(f"wlo{i}", [P, 2048], R) for i in range(SPLIT)]
        h = sb("h", [P, TT, D])
        gain_rows = sb("gain_rows", [4 * KB, P])
        gT = sb("gT", [P, 4 * KB])
        ident_r = sb("ident_r", [P, P], R)
        mask_r = sb("mask_r", [P, 64], R)
        consts = sb("consts_sb", [P, C_COLS])
        small_g = sb("small_g", [P, B_QL + B_KVL + C_DV])
        with ExitStack() as reuse:
            lam_in = sb("lam_in", [P, 4, C_DH], F, reuse)
        with ExitStack() as reuse:
            rt = sb("rt", [P, 10, TT, N_EXP], F, reuse)
        ctx.enter_context(nc.sbuf_tensor("hold_lam", [P, 4 * C_DH], F))
        xn = sb("xn", [P, TT, D])
        pos_i = sb("pos_i", [P, TT], I32)
        pos_f = sb("pos_f", [P, TT])
        with ExitStack() as reuse:
            trig = sb("trig", [P, 4, TT, N_FREQ], F, reuse)
        with ExitStack() as reuse:
            logT = sb("logT", [2 * N_EXP, S], F, reuse)
        ctx.enter_context(nc.sbuf_tensor("hold_trig", [P, 4 * TT * N_FREQ], F))
        cc = sb("cc", [P, TT, C_DH])
        ss = sb("ss", [P, TT, C_DH])
        minus_half = sb("minus_half", [P, 32])
        ssq = sb("ssq", [P, 32])
        ms = sb("ms", [P, 32])
        rstd = sb("rstd", [P, 32])
        lam = sb("lam", [P, 8])
        mx = sb("mx", [P, 24, 4])
        nmx = sb("nmx", [P, 24, 4])
        den = sb("den", [P, 24, 4])
        rden = sb("rden", [P, 24, 4])
        wr = sb("wr", [P, KB, N_EXP])
        wr2 = sb("wr2", [P, KB, 2 * N_EXP], R)
        ident = consts[:, C_ID:C_ID + P]
        tri = consts[:, C_TRI:C_TRI + P]
        ones = consts[:, C_ONES:C_ONES + P]
        iota = consts[:, C_IOTA:C_IOTA + P]
        mask = consts[:, C_MASK:C_MASK + 64]
        e8 = consts[:, C_E8:C_E8 + 8]
        r8 = consts[:, C_R8:C_R8 + 8]
        fold = consts[0:2 * N_EXP, C_FOLD:C_FOLD + 8]
        g_sub = small_g[:, B_QL + B_KVL:]

        with ExitStack() as reuse:
            xhi = sb("xhi", [P, KB, S], R, reuse)
            xlo = sb("xlo", [P, KB, S], R, reuse)
        with ExitStack() as reuse:
            qT = sb("qT", [P, KB, S], F, reuse)
            kT = sb("kT", [P, KB, S], F, reuse)
        with ExitStack() as reuse:
            ahead2 = sb("ahead2", [P, 2048], F, reuse)
        ctx.enter_context(nc.sbuf_tensor("hold_x", [P, 2 * KB * S], F))

        with ExitStack() as reuse:
            proj = sb("proj", [P, TT, EVEN_IN], F, reuse)
            qB = sb("qB", [P, TT, B_HEADS, B_QK], F, reuse)
            kB = sb("kB", [P, TT, B_HEADS, B_QK], F, reuse)
            vB = sb("vB", [P, TT, B_HEADS, B_V], F, reuse)
            qA = [sb(f"qA{i}", [P, 4, S], R, reuse) for i in range(2)]
            kA = [sb(f"kA{i}", [P, 4, S], R, reuse) for i in range(2)]
            bias = sb("bias", [P, A_HEADS, S], F, reuse)
            with ExitStack() as again:
                lat = sb("lat", [P, TT, B_QL + B_KVL], F, again)
                lhi = sb("lhi", [P, 3, S], R, again)
                llo = sb("llo", [P, 3, S], R, again)
                ropeB = sb("ropeB", [P, 4, TT, 16], F, again)
                ropeQ = sb("ropeQ", [P, 4, B_HEADS, 16], F, again)
            biased = [sb(f"biased{i}", [P, 384], F, reuse) for i in range(2)]
            probs = [sb(f"probs{i}", [P, 384], F, reuse) for i in range(2)]
            probsT = [sb(f"probsT{i}", [P, 384], F, reuse) for i in range(2)]
        with ExitStack() as reuse:
            act_g = sb("act_g", [P, TT, CH], F, reuse)
            hid = sb("hid", [P, TT, CH], F, reuse)
            hidhi = sb("hidhi", [P, 4, S], R, reuse)
            hidlo = sb("hidlo", [P, 4, S], R, reuse)
        with ExitStack() as reuse:
            vC = sb("vC", [P, TT, D], F, reuse)
            rotated = sb("rotated", [P, TT, D], F, reuse)
            qC = [sb(f"qC{i}", [P, KB, S], R, reuse) for i in range(2)]
            kC = [sb(f"kC{i}", [P, KB, S], R, reuse) for i in range(2)]
            with ExitStack() as again:
                rot = [sb(f"rot{i}", [P, CH], F, again) for i in range(2)]
            probs1 = [sb(f"probs1_{i}", [P, 2, 384], F, reuse) for i in range(2)]
            scaled2 = sb("scaled2", [P, 384], F, reuse)
            diff = [sb(f"diff{i}", [P, 384], F, reuse) for i in range(2)]
            diffT = [sb(f"diffT{i}", [P, 384], F, reuse) for i in range(2)]
            junk = sb("junk", [P, TT, C_DV], F, reuse)
        with ExitStack() as reuse:
            ahead = [sb(f"ahead{i}", [P, 2048], F, reuse) for i in range(2)] + [ahead2]
            gain = [sb(f"gain{i}", [P, D], F, reuse) for i in range(2)]
            thi = sb("thi", [P, TT, D], R, reuse)
            tlo = sb("tlo", [P, TT, D], R, reuse)
            xghi = sb("xghi", [P, KB, P], R, reuse)
            xglo = sb("xglo", [P, KB, P], R, reuse)
            act_e = sb("act_e", [P, CH], F, reuse)
            hid_e = sb("hid_e", [P, CH], F, reuse)
            hehi = sb("hehi", [P, 4, P], R, reuse)
            helo = sb("helo", [P, 4, P], R, reuse)
            yhi = sb("yhi", [P, D], R, reuse)
            ylo = sb("ylo", [P, D], R, reuse)
            sel = sb("sel", [P, TT, P], R, reuse)
            selT = sb("selT", [P, S], R, reuse)
            gcur = sb("gcur", [P, TT], F, reuse)
            gslot = sb("gslot", [P, 1], F, reuse)
            logit = sb("logit", [P, TT, 8], F, reuse)
            rs = sb("rs", [P, 16, TT], F, reuse)
            scan = sb("scan", [P, 4, 16], F, reuse)
            chosen = sb("chosen", [P, TT, 12], F, reuse)
            slot = sb("slot", [P, TT, 12], F, reuse)
            gate = sb("gate", [P, TT, 12], F, reuse)
            order = sb("order", [P, 16], F, reuse)
            order_i = sb("order_i", [P, 16], I32, reuse)

        ps = ctx.enter_context(nc.psum_tensor("ps", [P, 8, CH], F))

        s_x = sem("x_loaded")
        s_consts, s_small, s_bias_in, s_lam_in, s_wr_in, s_pos = [sem(n) for n in (
            "consts_loaded", "small_gains_loaded", "bias_loaded", "lambda_loaded", "router_loaded", "positions_loaded")]
        s_gain = [sem(f"gain_loaded{i}") for i in range(2)]
        s_rows, s_gfull, s_gT, s_fr = [sem(n) for n in ("gain_rows_loaded", "gains_transposed", "gains_ready", "constants_rounded")]
        s_raw = [sem(f"raw_loaded{i}") for i in range(RAW)]
        s_ahead = [sem(f"ahead_loaded{i}") for i in range(3)]
        s_hi, s_lo, s_used = sem("hi_ready"), sem("lo_ready"), sem("tile_used")
        full = [sem(f"bank_full{i}") for i in range(8)]
        free = [sem(f"bank_free{i}") for i in range(8)]
        s_sq, s_ms, s_rstd, s_xn = [sem(n) for n in ("squares_summed", "mean_ready", "rstd_ready", "normed")]
        s_hiT, s_loT = sem("left_hi_ready"), sem("left_lo_ready")
        s_dve, s_pool, s_const = sem("vector_step"), sem("pool_step"), sem("exponent_set")
        s_lat, s_rope, s_bias = [sem(n) for n in ("latents_normed", "rotated_b", "bias_masked")]
        s_trig, s_sin, s_lam = sem("angles_ready"), sem("sines_ready"), sem("lambda_terms")
        s_sc, s_nm, s_exp, s_diff = [sem(n) for n in ("scores_full", "maxima_ready", "exponentials_ready", "difference_ready")]
        s_ptf, s_pT, s_of, s_mix = [sem(n) for n in ("probsT_full", "probsT_ready", "head_full", "head_out")]
        s_qkhi, s_tab = sem("heads_hi_ready"), sem("tables_scaled")
        s_rot, s_sqc, s_sub = sem("rotated_c"), sem("head_squares"), sem("heads_normed")
        s_prn = sem("probs_over_sum")
        c_t, c_hi, c_lo = sem("headT_full"), sem("headT_hi"), sem("headT_lo")
        s_res = sem("residual_added")
        f_act, f_h, f_t, f_hhi, f_ht, f_d, f_add = [sem(n) for n in (
            "ffn_silu", "ffn_hidden", "ffn_hidT_full", "ffn_hidT_hi", "ffn_hidT_ready", "ffn_down_full", "ffn_down_added")]
        s_logT, s_logS = sem("logitsT_full"), sem("logitsT_ready")
        s_wr, s_log, s_dlt, s_ex, s_cho, s_rank, s_order = [sem(n) for n in (
            "router_split", "logits_full", "second_minus_first", "second_exp", "choice_ready", "ranks_full", "passes_ready")]
        s_tok, s_tlo = sem("tokens_hi"), sem("tokens_split")
        m_sel, m_aux, m_auxr, m_x, m_xhi, m_xlo, m_act, m_h, m_t, m_thi, m_tr, m_yhi, m_ylo, m_acc, m_add = [
            sem(n) for n in (
                "selection_ready", "selT_full", "selT_ready", "gather_full", "gather_hi", "gather_ready",
                "silu_ready", "hidden_ready", "hidT_full", "hidT_hi", "hidT_ready",
                "expert_out_hi", "expert_out_ready", "scatter_full", "scatter_added")]
        last_hi, last_lo = sem("last_out_hi"), sem("last_out_ready")
        last_acc, last_add = sem("last_scatter_full"), sem("last_scatter_added")
        LAST_BANKS = (6, 7, 0, 1)
        s_fin, s_out = sem("final_normed"), sem("stored")

        use, uses, fulls = {}, [0] * 8, [0] * 8

        def plan(key, bank, counted=True):
            use[key] = (bank, fulls[bank], uses[bank])
            fulls[bank] += 1
            uses[bank] += counted

        def plan_left(stage):
            for g in range(4):
                plan(("left", stage, g), 4 + g, counted=False)

        def plan_columns(stage, c, pair):
            for t in range(TT):
                plan((stage, c, t), 2 * pair + t, counted=stage[:3] != "out")

        def plan_heads(name, groups, first=4):
            for g in range(groups):
                plan((name, g), first + g)

        UNITS0, UNITS = A_HEADS + B_HEADS, A_HEADS + B_HEADS + C_HEADS
        plan_left(0)
        plan_columns("in0", 3, 0)
        plan_columns("in0", 0, 1)
        plan("lat0", 4, counted=False)
        plan("lat1", 5, counted=False)
        plan_columns("in0", 1, 0)
        plan_columns("uq", 0, 1)
        plan_columns("uq", 1, 0)
        plan_columns("ukv", 0, 1)
        plan_columns("ukv", 1, 0)
        plan_heads("qA", 2)
        plan_heads("kA", 2, 6)
        plan_columns("in0", 2, 1)
        plan_heads("qB", 4)
        plan_heads("kB", 4)
        before_units0 = list(uses)
        plan_columns("out0", 0, 0)
        plan_columns("out0", 1, 1)
        plan_left(2)
        plan_left(3)
        for c in range(6):
            plan_columns("in1", c, c % 2)
            if c == 2:
                plan_heads("qC", 4)
            if c == 4:
                plan_heads("kC", 4)
        before_units1 = list(uses)
        plan_columns("out1", 0, 0)
        plan_columns("out1", 1, 1)
        plan_left(5)

        def wait_full(eng, key):
            eng.wait_ge(full[use[key][0]], use[key][1] + 1)

        def wait_free(eng, key):
            eng.wait_ge(free[use[key][0]], use[key][2] + 1)

        def bank(key):
            return ps[:, use[key][0], :]

        def spread(ap, shape, axis):
            return ap.unsqueeze(axis).to_broadcast(shape)

        def raw_count(n):
            return 16 * (n // RAW + 1)

        def width_of(n):
            return {0: 1664, 1: 1664, T_UQ: 1536, T_UKV: 1024}.get(n, 2048)

        MIX0, FFN0, MIX1, FFN1, FINAL = range(5)
        LAT, SUBLN = 10, 16
        SQ = {MIX0: 2, FFN0: 8, MIX1: 10, FFN1: 12, FINAL: 14}
        LEFT = {0: 4, 1: 10, 2: 14, 3: 18, 5: 22}
        GAIN = {0: MIX0, 2: FFN0, 3: MIX1, 5: FFN1}
        G_COL = {MIX0: 0, MIX1: KB, FFN0: 2 * KB, FFN1: 3 * KB}
        RSTD = {MIX0: 1, FFN0: 3, MIX1: 4, FFN1: 5 + C_HEADS, FINAL: 6 + C_HEADS}
        LAST = N_FULL
        T_LAST = T_FFN + 6 * N_FULL - 2
        block = ctx.enter_context(nc.Block())

        @block.sync
        def _(sp):
            for t in range(TT):
                sp.dma_start(h[:, t, :], a["x"][0, t * P:(t + 1) * P, :]).then_inc(s_x, 16)

            def load(n, dst_shape, src):
                if n >= RAW:
                    sp.wait_ge(s_lo, n - RAW + 1)
                k, m = dst_shape
                dst = raw[n % RAW][:, 0:k * m].rearrange("p (k m) -> p k m", k=k)
                sp.dma_start(dst, src).then_inc(s_raw[n % RAW], 16)

            for i, c in enumerate(IN0_ORDER[:3]):
                width = min(CH, EVEN_IN - c * CH)
                for b in range(2):
                    load(T_IN0 + 2 * i + b, (4, width), w_in0[:, 4 * b:4 * b + 4, c * CH:c * CH + width])
            load(T_UQ, (2, 768), w_uq)
            load(T_UKV, (1, D), w_ukv.rearrange("p (k n) -> p k n", k=1))
            for b in range(2):
                load(T_IN0V + b, (4, CH), w_in0[:, 4 * b:4 * b + 4, 2 * CH:3 * CH])
            for c in range(2):
                for b in range(2):
                    load(T_OUT0 + 2 * c + b, (4, CH), w_out0[:, 4 * b:4 * b + 4, c * CH:(c + 1) * CH])
            for half in range(2):
                for b in range(2):
                    load(T_FFN + 2 * half + b, (4, CH), w_gu[:, 4 * b:4 * b + 4, half * FF_DENSE:half * FF_DENSE + CH])
            with sp.Fori(1, N_FULL) as j:
                for r in range(6):
                    n = T_FFN + 4 + r
                    sp.wait_ge(s_lo, (j - 1) * 6 + (n - RAW + 1))
                    dst = raw[n % RAW][:, :].rearrange("p (k m) -> p k m", k=4)
                    if r < 4:
                        half, b = r // 2, r % 2
                        src = w_gu[:, 4 * b:4 * b + 4, ds(j * CH + half * FF_DENSE, CH)]
                    else:
                        src = w_dn[:, ds(j * 4 - 4, 4), (r - 4) * CH:(r - 3) * CH]
                    sp.dma_start(dst, src).then_inc(s_raw[n % RAW], 16)
            n = T_FFN + 6 * N_FULL - 2
            rest = FF_DENSE - N_FULL * CH
            for half in range(2):
                at = half * FF_DENSE + N_FULL * CH
                load(n + half, (8, rest), w_gu[:, :, at:at + rest])
            for half in range(2):
                load(n + 2 + half, (4, CH), w_dn[:, 4 * N_FULL - 4:4 * N_FULL, half * CH:(half + 1) * CH])
            load(n + 4, (2, D), w_dn[:, 4 * N_FULL:4 * N_FULL + 2, :])
            for c in range(6):
                for b in range(2):
                    load(T_IN1 + 2 * c + b, (4, CH), w_in1[:, 4 * b:4 * b + 4, c * CH:(c + 1) * CH])
            for c in range(2):
                for b in range(2):
                    load(T_OUT1 + 2 * c + b, (4, CH), w_out1[:, 4 * b:4 * b + 4, c * CH:(c + 1) * CH])

            def gu(e, half, b, at):
                return e_gu[ds(e, 1), :, 4 * b:4 * b + 4, ds(at + half * FF_EXP, CH)].rearrange("e p k n -> (e p) k n")

            def dn(e, k, half):
                return e_dn[ds(e, 1), :, ds(k, 4), half * CH:(half + 1) * CH].rearrange("e p k n -> (e p) k n")

            def tile_of(e, j, r):
                return gu(e, r // 2, r % 2, j * CH) if r < 4 else dn(e, j * 4 - 4, r - 4)

            def put(i, src, free_at, dst=None, signal=None):
                if free_at is not None:
                    sp.wait_ge(s_lo, free_at)
                n_slot = (T_MOE + i) % RAW
                dst = raw[n_slot] if dst is None else dst
                sp.dma_start(dst[:, :].rearrange("p (k m) -> p k m", k=4), src).then_inc(signal or s_raw[n_slot], 16)

            def turns(first, e, j0):
                with sp.Fori(j0, M_CH) as j:
                    for r in range(6):
                        put(4 + r, tile_of(e, j, r), (j - 1) * 6 + first + (4 + r - RAW + 1))
                for half in range(2):
                    put(M_TILES - 2 + half, dn(e, 4 * M_CH - 4, half), first + (M_TILES - 2 + half - RAW + 1))

            def put0(i, free_at, **to):
                j, r = (0, i) if i < 4 else (1 + (i - 4) // 6, (i - 4) % 6)
                put(i, tile_of(0, j, r), free_at, **to)

            for i in range(6):
                put0(i, T_MOE + i - RAW + 1)
            sp.wait_ge(c_lo, C_HEADS - 1)
            for i in (9, 10):
                put0(i, None, dst=ahead[i - 9], signal=s_ahead[i - 9])
            for i in (6, 7):
                put0(i, T_MOE + i - RAW + 1)
            sp.wait_ge(s_logT, 1)
            put0(11, None, dst=ahead[2], signal=s_ahead[2])
            put0(8, T_MOE + 8 - RAW + 1)
            for i in (15, 16, 17):
                put0(i, T_MOE + i - 2 * RAW + 1)
            for i in (12, 13, 14, 18, 19, 20, 21):
                put0(i, T_MOE + i - RAW + 1)
            turns(T_MOE, 0, 4)
            sp.wait_ge(s_order, 1)
            passes = sp.value_load(order_i[0:1, 15:16], min_val=N_EXP, max_val=MAX_PASS)
            with sp.Fori(1, passes) as p:
                e = sp.value_load(order_i[0:1, ds(p, 1)], min_val=0, max_val=N_EXP - 1)
                first = p * M_TILES + T_MOE
                for i in range(4):
                    put(i, gu(e, i // 2, i % 2, 0), first + (i - RAW + 1))
                turns(first, e, 1)
            sp.wait_ge(s_fin, 2)
            for t in range(TT):
                sp.dma_start(a["out"][0, t * P:(t + 1) * P, :], xn[:, t, :]).then_inc(s_out, 16)
            sp.wait_ge(s_out, 16 * TT)

        @block.scalar
        def _(act):
            done = [0]

            act.dma_start(consts[:], a["consts"]).then_inc(s_consts, 16)
            for i, name in enumerate(("mix_norm_g", "ffn_norm_g")):
                act.dma_start(gain_rows[2 * KB * i:2 * KB * (i + 1), :],
                              a[name].rearrange("a (k p) -> (a k) p", p=P)).then_inc(s_rows, 16)
            act.dma_start(small_g[:, 0:B_QL], a["q_norm_b"][0:1, :].to_broadcast([P, B_QL])).then_inc(s_small, 16)
            act.dma_start(small_g[:, B_QL:B_QL + B_KVL],
                          a["kv_norm_b"][0:1, :].to_broadcast([P, B_KVL])).then_inc(s_small, 16)
            act.dma_start(g_sub, a["subln_g"][0:1, :].to_broadcast([P, C_DV])).then_inc(s_small, 16)
            with nc.allow_non_contiguous_dma(reason="256 positions, the router's short rows"):
                act.dma_start(pos_i[:], a["positions"].rearrange("a (t p) -> p (a t)", p=P)).then_inc(s_pos, 16)
                act.dma_start(wr[:], a["w_router"][0].rearrange("(k p) n -> p k n", p=P)).then_inc(s_wr_in, 16)

            def split(n):
                act.wait_ge(s_raw[n % RAW], raw_count(n))
                if n >= SPLIT:
                    act.wait_ge(s_used, n - SPLIT + 1)
                w = width_of(n)
                nc.scalar.activation(whi[n % SPLIT][:, 0:w], raw[n % RAW][:, 0:w], ACT.Copy).then_inc(s_hi, 1)

            def upto(n):
                while done[0] <= n:
                    split(done[0])
                    done[0] += 1

            def squares(k):
                for t in range(TT):
                    nc.scalar.activation(xn[:, t, :], h[:, t, :], ACT.Square,
                                         accum_out=ssq[:, 2 * k + t:2 * k + t + 1]).then_inc(s_sq, 1)

            def left_hi(stage, groups=range(4)):
                for g in groups:
                    wait_full(act, ("left", stage, g))
                    if stage in GAIN:
                        for i in range(2):
                            col = G_COL[GAIN[stage]] + 2 * g + i
                            last = nc.scalar.activation(xhi[:, 2 * g + i, :], bank(("left", stage, g))[:, i * S:(i + 1) * S],
                                                        ACT.Copy, scale=gT[:, col:col + 1])
                        last.then_inc(s_hiT, 1)
                        continue
                    nc.scalar.activation(xhi[:, 2 * g:2 * g + 2, :], bank(("left", stage, g)).rearrange(
                        "p (k s) -> p k s", k=2), ACT.Copy).then_inc(s_hiT, 1)

            def copy_out(key, dst, src=None, scale=1.0):
                nc.scalar.activation(dst, bank(key) if src is None else src, ACT.Copy,
                                     scale=scale).then_inc(free[use[key][0]], 1)

            def scale_of(k, t):
                return rstd[:, 2 * k + t:2 * k + t + 1]

            def heads_hi(name, dst, groups):
                for g in range(groups):
                    wait_full(act, (name, g))
                    nc.scalar.activation(dst[:, 2 * g:2 * g + 2, :].rearrange("p k s -> p (k s)"), bank((name, g)),
                                         ACT.Copy).then_inc(s_qkhi, 1)

            act.wait_ge(s_consts, 16)
            nc.scalar.activation(ident_r[:], ident, ACT.Copy)
            nc.scalar.activation(mask_r[:], mask, ACT.Copy).then_inc(s_fr, 1)
            act.wait_ge(s_gT, 1)
            left_hi(0, (0, 1))
            upto(0)
            left_hi(0, (2, 3))
            upto(1)
            squares(MIX0)
            upto(3)
            act.wait_ge(s_used, T_IN0 + 2)
            act.wait_ge(s_rstd, RSTD[MIX0])
            for t in range(TT):
                copy_out(("in0", 3, t), proj[:, t, 1536:EVEN_IN], bank(("in0", 3, t))[:, 0:416], scale_of(MIX0, t))
            for t in range(TT):
                wait_free(act, ("in0", 3, t))
            for t in range(TT):
                for c0, c1 in ((0, B_QL), (B_QL, B_QL + B_KVL)):
                    col = LAT + 2 * t + (c0 > 0)
                    nc.scalar.activation(lat[:, t, c0:c1], proj[:, t, 1536 + c0:1536 + c1], ACT.Square,
                                         accum_out=ssq[:, col:col + 1]).then_inc(s_sq, 1)
            upto(4)
            for hd in range(A_HEADS):
                row = a["rel_bias_a"][0, hd:hd + 1, P + 1:P + 1 + S]
                act.dma_start(bias[:, hd, :], bass.AP(row.tensor, row.offset, [[1, P], [1, S]])).then_inc(s_bias_in, 16)
            for i, name in enumerate(("lambda_q1", "lambda_k1", "lambda_q2", "lambda_k2")):
                act.dma_start(lam_in[:, i, :], a[name][0:1, :].to_broadcast([P, C_DH])).then_inc(s_lam_in, 16)
            upto(5)
            act.wait_ge(s_used, T_IN0 + 4)
            for t in range(TT):
                copy_out(("in0", 0, t), proj[:, t, 0:CH], scale=scale_of(MIX0, t))
            wait_full(act, "lat0")
            nc.scalar.activation(lhi[:, 0:2, :], bank("lat0").rearrange("p (k s) -> p k s", k=2), ACT.Copy).then_inc(s_hiT, 1)
            wait_full(act, "lat1")
            nc.scalar.activation(lhi[:, 2, :], bank("lat1")[:, 0:S], ACT.Copy).then_inc(s_hiT, 1)
            act.wait_ge(s_trig, 2)
            nc.scalar.activation(trig[:, 3, :, :], trig[:, 0, :, :], ACT.Sin).then_inc(s_sin, 1)
            nc.scalar.activation(trig[:, 2, :, :], trig[:, 1, :, :], ACT.Sin).then_inc(s_sin, 1)
            upto(7)
            act.wait_ge(s_used, T_IN0 + 6)
            for t in range(TT):
                copy_out(("in0", 1, t), proj[:, t, CH:2 * CH], scale=scale_of(MIX0, t))
            upto(8)
            act.wait_ge(s_used, T_UQ + 1)
            for c, w in ((0, CH), (1, 768 - CH)):
                for t in range(TT):
                    copy_out(("uq", c, t), qB[:, t, :, :].rearrange("p a b -> p (a b)")[:, c * CH:c * CH + w],
                             bank(("uq", c, t))[:, 0:w])
            upto(9)
            act.wait_ge(s_used, T_UKV + 1)
            for c in range(2):
                for t in range(TT):
                    src = bank(("ukv", c, t)).rearrange("p (a b) -> p a b", a=4)
                    nc.scalar.activation(kB[:, t, 4 * c:4 * c + 4, 0:B_NOPE], src[:, :, 0:B_NOPE], ACT.Copy)
                    copy_out(("ukv", c, t), vB[:, t, 4 * c:4 * c + 4, :], src[:, :, B_NOPE:])
            heads_hi("qA", qA[0], 2)
            heads_hi("kA", kA[0], 2)
            upto(11)
            act.wait_ge(s_used, T_IN0V + 2)
            for t in range(TT):
                copy_out(("in0", 2, t), proj[:, t, 2 * CH:3 * CH], scale=scale_of(MIX0, t))
            for g in range(4):
                wait_full(act, ("qB", g))
                copy_out(("qB", g), qT[0:B_QK, 2 * g:2 * g + 2, :].rearrange("p k s -> p (k s)"),
                         ps[0:B_QK, use[("qB", g)][0], :])

            def exponentials(u):
                act.wait_ge(s_nm, u + 1)
                if u < UNITS0 and u >= 2:
                    act.wait_ge(s_ptf, u - 1)
                if u >= UNITS0 + 2:
                    act.wait_ge(s_diff, u - UNITS0 - 1)
                for m in range(1 if u < UNITS0 else 2):
                    for t, (c0, c1) in enumerate(((0, 128), (128, 384))):
                        col = 2 * m + t
                        src = biased[u % 2][:, c0:c1] if u < A_HEADS else ps[:, 2 * (u % 2) + m, c0:c1]
                        dst = probs[u % 2][:, c0:c1] if u < UNITS0 else probs1[u % 2][:, m, c0:c1]
                        last = nc.scalar.activation(
                            dst, src, ACT.Exp, bias=nmx[:, u, col:col + 1],
                            scale=1.0 if u < A_HEADS else B_SCALE if u < UNITS0 else C_SCALE,
                            accum_out=den[:, u, col:col + 1])
                last.then_inc(s_exp, 1)

            def probs_out(u, dst):
                act.wait_ge(s_ptf, u + 1)
                if u >= 2:
                    act.wait_ge(s_of, u - 1)
                nc.scalar.activation(dst[u % 2][:, :], ps[:, 4 + u % 2, 0:384], ACT.Copy).then_inc(s_pT, 1)

            def left1_hi(groups):
                for g in groups:
                    act.wait_ge(s_mix, 4 * g + 4)
                    nc.scalar.activation(xhi[:, 2 * g:2 * g + 2, :].rearrange("p k s -> p (k s)"),
                                         xn[:, g // 2, g % 2 * CH:(g % 2 + 1) * CH], ACT.Copy).then_inc(s_hiT, 1)

            exponentials(0)
            for u in range(UNITS0):
                if u + 1 < UNITS0:
                    exponentials(u + 1)
                probs_out(u, probsT)
                if u == UNITS0 - 2:
                    left1_hi((0, 1, 2))
            left1_hi((3,))
            upto(15)
            left_hi(2)
            squares(FFN0)
            upto(T_FFN + 3)

            def silu(j, width):
                for t in range(TT):
                    last = nc.scalar.activation(act_g[:, t, 0:width], ps[:, t, 0:width], ACT.Silu, scale=scale_of(FFN0, t))
                last.then_inc(f_act, 1)

            def hid_hi(j, k=4):
                act.wait_ge(f_t, j + 1)
                nc.scalar.activation(hidhi[:, 0:k, :], ps[:, 4:6, :].rearrange("p b (k s) -> p (b k) s", k=2)[:, 0:k, :],
                                     ACT.Copy).then_inc(f_hhi, 1)

            act.wait_ge(s_used, T_FFN + 2)
            act.wait_ge(s_rstd, RSTD[FFN0])
            silu(0, CH)
            upto(T_FFN + 5)
            with act.Fori(1, N_FULL) as j:
                def split_next(r):
                    n = T_FFN + 4 + r
                    act.wait_ge(s_raw[n % RAW], (j - 1) * 16 + raw_count(n))
                    act.wait_ge(s_used, (j - 1) * 6 + (n - SPLIT + 1))
                    nc.scalar.activation(whi[n % SPLIT][:, :], raw[n % RAW][:, :], ACT.Copy).then_inc(s_hi, 1)

                split_next(2)
                split_next(3)
                act.wait_ge(s_used, (j - 1) * 6 + (T_FFN + 6))
                act.wait_ge(f_h, j * 1)
                silu(j, CH)
                hid_hi(j - 1)
                for r in range(4, 8):
                    split_next(r)
            done[0] = T_LAST + 2
            upto(T_LAST + 2)
            act.wait_ge(s_used, T_LAST + 1)
            act.wait_ge(f_h, LAST)
            silu(LAST, 256)
            hid_hi(LAST - 1)
            upto(T_LAST + 5)
            hid_hi(LAST, 2)
            upto(T_LAST + 6)
            left_hi(3)
            squares(MIX1)

            act.wait_ge(s_lam, 1)
            nc.scalar.activation(lam[:, 2:4], lam[:, 0:2], ACT.Exp).then_inc(s_lam, 1)
            act.wait_ge(s_wr_in, 16)
            nc.scalar.activation(wr2[:, :, 0:N_EXP], wr[:], ACT.Copy).then_inc(s_wr, 1)
            upto(T_IN1 + 7)
            heads_hi("qC", qC[0], 4)
            upto(T_IN1 + 11)
            act.wait_ge(s_used, T_IN1 + 10)
            act.wait_ge(s_rstd, RSTD[MIX1])
            for t in range(TT):
                copy_out(("in1", 4, t), vC[:, t, 0:CH], scale=scale_of(MIX1, t))
            heads_hi("kC", kC[0], 4)
            upto(T_IN1 + 13)
            act.wait_ge(s_used, T_IN1 + 12)
            for t in range(TT):
                copy_out(("in1", 5, t), vC[:, t, CH:2 * CH], scale=scale_of(MIX1, t))
            exponentials(UNITS0)
            for i in range(C_HEADS + 1):
                u = UNITS0 + i
                if u + 1 < UNITS:
                    exponentials(u + 1)
                if u < UNITS:
                    probs_out(u, diffT)
                if i:
                    hd = i - 1
                    act.wait_ge(s_mix, u)
                    if hd:
                        act.wait_ge(s_sqc, hd)
                    for t in range(TT):
                        col = SUBLN + C_HEADS * t + hd
                        last = nc.scalar.activation(junk[:, t, :], xn[:, t, hd * C_DV:(hd + 1) * C_DV], ACT.Square,
                                                    accum_out=ssq[:, col:col + 1])
                    last.then_inc(s_sqc, 1)
                if i >= 4:
                    nc.scalar.activation(xhi[:, i - 4, :], ps[:, 6 + (u - 1) % 2, S:2 * S], ACT.Copy).then_inc(c_hi, 1)
            for i, n in enumerate((2, 1)):
                act.wait_ge(c_t, i + 1)
                nc.scalar.activation(xhi[:, C_HEADS - 3 + 2 * i:C_HEADS - 3 + 2 * i + n, :].rearrange("p k s -> p (k s)"),
                                     ps[:, 4 + i, 0:n * S], ACT.Copy).then_inc(c_hi, 1)
            act.dma_start(gain[0][:], a["ffn_norm_g"][1:2, :].to_broadcast([P, D])).then_inc(s_gain[0], 16)
            act.dma_start(gain[1][:], a["final_norm_g"].rearrange("(a n) -> a n", a=1).to_broadcast([P, D])).then_inc(s_gain[1], 16)
            upto(T_MOE + 1)
            left_hi(5)
            squares(FFN1)
            for t in range(TT):
                act.wait_ge(s_xn, t + 1)
                nc.scalar.activation(thi[:, t, :], xn[:, t, :], ACT.Copy).then_inc(s_tok, 1)
            act.wait_ge(s_dlt, 1)
            nc.scalar.activation(rs[:, 5, :], rs[:, 4, :], ACT.Exp).then_inc(s_ex, 1)
            upto(T_MOE + 2)

            def gathered_hi(p):
                act.wait_ge(m_x, p + 1)
                nc.scalar.activation(xghi[:], ps[:, 6:8, :].rearrange("p b (k s) -> p (b k) s", k=4),
                                     ACT.Copy).then_inc(m_xhi, 1)

            def output_hi(p):
                act.wait_ge(m_auxr, p + 1)
                act.wait_ge(s_used, p * M_TILES + (T_MOE + M_TILES))
                nc.scalar.activation(yhi[:], ps[:, 3:5, :].rearrange("p b n -> p (b n)"), ACT.Copy,
                                     scale=gslot[:, 0:1]).then_inc(m_yhi, 1)

            def expert_pass(p, first):
                def split_tile(i, turns=0, beside=False):
                    n = T_MOE + i
                    src = raw[n % RAW]
                    if beside and i >= 9:
                        act.wait_ge(s_ahead[i - 9], 16)
                        src = ahead[i - 9]
                    else:
                        less = 0 if first and i < 6 or i % 6 < 3 else 16
                        act.wait_ge(s_raw[n % RAW], p * (16 * M_CH) + turns * 16 + (raw_count(n) - less))
                    act.wait_ge(s_used, p * M_TILES + turns * 6 + (n - SPLIT + 1))
                    nc.scalar.activation(whi[n % SPLIT][:, :], src[:, :], ACT.Copy).then_inc(s_hi, 1)

                def silu_e():
                    nc.scalar.activation(act_e[:], ps[:, 0, :], ACT.Silu).then_inc(m_act, 1)

                def hid_hi_e(j):
                    act.wait_ge(m_t, p * M_CH + j + 1)
                    nc.scalar.activation(hehi[:], ps[:, 2, :].rearrange("p (k s) -> p k s", k=4),
                                         ACT.Copy).then_inc(m_thi, 1)

                if not first:
                    for i in range(3):
                        split_tile(i)
                    output_hi(p - 1)
                split_tile(3)
                act.wait_ge(s_used, p * M_TILES + (T_MOE + 2))
                silu_e()
                split_tile(4)
                split_tile(5)
                def turn(j, turns, beside=False):
                    split_tile(6, turns)
                    split_tile(7, turns)
                    act.wait_ge(s_used, p * M_TILES + j * 6 + T_MOE)
                    act.wait_ge(m_h, p * M_CH + j)
                    silu_e()
                    hid_hi_e(j - 1)
                    for i in range(8, 12):
                        split_tile(i, turns, beside)

                if first:
                    turn(1, 0, True)
                with act.Fori(2 if first else 1, M_CH) as j:
                    turn(j, j - 1)
                hid_hi_e(M_CH - 1)
                gathered_hi(p + 1)

            gathered_hi(0)
            expert_pass(0, True)
            act.wait_ge(s_order, 1)
            passes = act.value_load(order_i[0:1, 15:16], min_val=N_EXP, max_val=MAX_PASS)
            with act.Fori(1, passes) as p:
                expert_pass(p, False)
            act.wait_ge(m_auxr, passes * 1)
            for half in range(2):
                act.wait_ge(s_used, passes * M_TILES + (T_MOE - 1 + half))
                nc.scalar.activation(yhi[:, half * CH:(half + 1) * CH], ps[:, 3 + half, :], ACT.Copy,
                                     scale=gslot[:, 0:1]).then_inc(last_hi, 1)
            for t in range(TT):
                act.wait_ge(last_add, 3 + t)
                nc.scalar.activation(xn[:, t, :], h[:, t, :], ACT.Square,
                                     accum_out=ssq[:, 2 * FINAL + t:2 * FINAL + t + 1]).then_inc(s_sq, 1)

        @block.gpsimd
        def _(pool):
            steps = [0]

            def step(i):
                i.then_inc(s_pool, 1)
                steps[0] += 1

            def settle():
                pool.wait_ge(s_pool, steps[0])

            def rsqrt(count, c0, n, stride=1):
                cols = slice(c0, c0 + (n - 1) * stride + 1, stride)
                pool.wait_ge(s_ms, count)
                pool.tensor_tensor(rstd[:, cols], ms[:, cols], minus_half[:, 0:n], ALU.pow).then_inc(s_rstd, 1)

            pool.memset(minus_half[:], -0.5).then_inc(s_const, 1)
            pool.wait_ge(s_const, 1)
            rsqrt(1, 0, 2)
            rsqrt(2, LAT, 4)
            pool.wait_ge(s_bias_in, 16 * A_HEADS)
            pool.wait_ge(s_consts, 16)
            pool.tensor_tensor(bias[0:64, :, 0:64], bias[0:64, :, 0:64],
                               spread(mask[0:64, :], [64, A_HEADS, 64], 1), ALU.add).then_inc(s_bias, 1)
            pool.wait_ge(s_sin, 2)
            for half in range(2):
                cols = slice(32 * half, 32 * half + 32)
                step(pool.tensor_copy(cc[:, :, cols], trig[:, 2, :, 16:48]))
                step(pool.tensor_scalar(ss[:, :, cols], trig[:, 3, :, 16:48], 2.0 * half - 1.0, None, ALU.mult))
            settle()
            for t in range(TT):
                wait_free(pool, ("in0", 3, t))
            x1, x2 = proj[:, :, 1920:1936], proj[:, :, 1936:1952]
            cos, sin = trig[:, 2, :, 0:16], trig[:, 3, :, 0:16]
            for i, (x, y) in enumerate(((x1, cos), (x2, sin), (x1, sin), (x2, cos))):
                step(pool.tensor_tensor(ropeB[:, i, :, :], x, y, ALU.mult))
            settle()
            step(pool.tensor_tensor(ropeB[:, 0, :, :], ropeB[:, 0, :, :], ropeB[:, 1, :, :], ALU.subtract))
            step(pool.tensor_tensor(ropeB[:, 2, :, :], ropeB[:, 2, :, :], ropeB[:, 3, :, :], ALU.add))
            settle()
            for t in range(TT):
                for half in range(2):
                    at = B_NOPE + 16 * half
                    pool.tensor_copy(kB[:, t, :, at:at + 16],
                                     spread(ropeB[:, 2 * half, t, :], [P, B_HEADS, 16], 1)).then_inc(s_rope, 1)
            for c in range(2):
                for t in range(TT):
                    wait_free(pool, ("uq", c, t))
            for t in range(TT):
                x1, x2 = qB[:, t, :, 64:80], qB[:, t, :, 80:96]
                c, s = [spread(trig[:, i, t, 0:16], [P, B_HEADS, 16], 1) for i in (2, 3)]
                for i, (x, y) in enumerate(((x1, c), (x2, s), (x1, s), (x2, c))):
                    step(pool.tensor_tensor(ropeQ[:, i, :, :], x, y, ALU.mult))
                settle()
                pool.tensor_tensor(x1, ropeQ[:, 0, :, :], ropeQ[:, 1, :, :], ALU.subtract).then_inc(s_rope, 1)
                pool.tensor_tensor(x2, ropeQ[:, 2, :, :], ropeQ[:, 3, :, :], ALU.add).then_inc(s_rope, 1)
                pool.wait_ge(s_rope, 4 + 2 * (t + 1))
            rsqrt(3, 2 * FFN0, 2)
            rsqrt(4, 2 * MIX1, 2)
            pool.wait_ge(s_rstd, 4)
            for table in (cc, ss):
                for t in range(TT):
                    pool.tensor_scalar(table[:, t, :], table[:, t, :], rstd[:, 2 * MIX1 + t:2 * MIX1 + t + 1], None,
                                       ALU.mult).then_inc(s_tab, 1)
            for hd in range(C_HEADS):
                rsqrt(5 + hd, SUBLN + hd, TT, C_HEADS)
                pool.wait_ge(s_rstd, RSTD[MIX1] + 1 + hd)
                for t in range(TT):
                    head = xn[:, t, hd * C_DV:(hd + 1) * C_DV]
                    col = SUBLN + C_HEADS * t + hd
                    step(pool.tensor_scalar(head, head, rstd[:, col:col + 1], None, ALU.mult))
                settle()
                heads = xn[:, :, hd * C_DV:(hd + 1) * C_DV]
                pool.tensor_tensor(heads, heads, spread(g_sub, [P, TT, C_DV], 1), ALU.mult).then_inc(s_sub, 1)
            rsqrt(5 + C_HEADS, 2 * FFN1, 2)
            for t in range(TT):
                pool.wait_ge(s_tok, t + 1)
                pool.tensor_tensor(tlo[:, t, :], xn[:, t, :], thi[:, t, :].bitcast(F), ALU.subtract).then_inc(s_tlo, 1)
            rsqrt(6 + C_HEADS, 2 * FINAL, 2)

        @block.vector
        def _(dve):
            done, steps = [0], [0]

            def step(i):
                i.then_inc(s_dve, 1)
                steps[0] += 1

            def settle():
                dve.wait_ge(s_dve, steps[0])

            def upto(n):
                while done[0] <= n:
                    m = done[0]
                    dve.wait_ge(s_hi, m + 1)
                    w = width_of(m)
                    dve.tensor_tensor(wlo[m % SPLIT][:, 0:w], raw[m % RAW][:, 0:w], whi[m % SPLIT][:, 0:w].bitcast(F),
                                      ALU.subtract).then_inc(s_lo, 1)
                    done[0] += 1

            def mean(c0, n, width, stride=1):
                cols = slice(c0, c0 + (n - 1) * stride + 1, stride)
                return dve.tensor_scalar(ms[:, cols], ssq[:, cols],
                                         1.0 / width, EPS, ALU.mult, ALU.add)

            def rstd_of(k):
                dve.wait_ge(s_sq, SQ[k])
                mean(2 * k, 2, D).then_inc(s_ms, 1)

            def norm(k, gains, done_sem):
                dve.wait_ge(s_rstd, RSTD[k])
                dve.wait_ge(s_gain[gains], 16)
                for t in range(TT):
                    dve.scalar_tensor_tensor(xn[:, t, :], h[:, t, :], rstd[:, 2 * k + t:2 * k + t + 1], gain[gains][:, :],
                                             ALU.mult, ALU.mult).then_inc(done_sem, 1)

            def left_lo(stage, groups=range(4)):
                for g in groups:
                    dve.wait_ge(s_hiT, LEFT[stage] - 3 + g)
                    key = ("left", stage, g)
                    if stage in GAIN:
                        for i in range(2):
                            col = G_COL[GAIN[stage]] + 2 * g + i
                            last = dve.scalar_tensor_tensor(xlo[:, 2 * g + i, :], bank(key)[:, i * S:(i + 1) * S], gT[:, col:col + 1],
                                                            xhi[:, 2 * g + i, :].bitcast(F), ALU.mult, ALU.subtract)
                        last.then_inc(s_loT, 1)
                        continue
                    dve.tensor_tensor(xlo[:, 2 * g:2 * g + 2, :], bank(key).rearrange("p (k s) -> p k s", k=2),
                                      xhi[:, 2 * g:2 * g + 2, :].bitcast(F), ALU.subtract).then_inc(s_loT, 1)

            def heads_lo(name, dst, groups, first):
                for g in range(groups):
                    dve.wait_ge(s_qkhi, first + g + 1)
                    dve.tensor_tensor(dst[1][:, 2 * g:2 * g + 2, :].rearrange("p k s -> p (k s)"), bank((name, g)),
                                      dst[0][:, 2 * g:2 * g + 2, :].rearrange("p k s -> p (k s)").bitcast(F),
                                      ALU.subtract).then_inc(free[use[(name, g)][0]], 1)

            def add_columns(stage, c):
                for t in range(TT):
                    part = h[:, t, c * CH:(c + 1) * CH]
                    dve.tensor_tensor(part, part, bank((stage, c, t)), ALU.add).then_inc(s_res, 1)

            dve.wait_ge(s_gfull, 1)
            dve.tensor_copy(gT[:], ps[:, 0, 0:4 * KB]).then_inc(s_gT, 1)
            left_lo(0, (0, 1))
            upto(0)
            left_lo(0, (2, 3))
            upto(1)
            rstd_of(MIX0)
            upto(2)
            dve.wait_ge(s_consts, 16)
            dve.wait_ge(s_pos, 16)
            step(dve.tensor_copy(pos_f[:], pos_i[:]))
            settle()
            for t in range(TT):
                step(dve.tensor_scalar(trig[:, 0, t, :], consts[:, C_FREQ:C_FREQ + N_FREQ], pos_f[:, t:t + 1], None, ALU.mult))
            settle()
            step(dve.tensor_scalar(trig[:, 1, :, :], trig[:, 0, :, :], 1.0 / TWO_PI, ROUND, ALU.mult, ALU.add))
            settle()
            step(dve.tensor_scalar(trig[:, 1, :, :], trig[:, 1, :, :], ROUND, None, ALU.subtract))
            settle()
            for part in TURN_PARTS:
                step(dve.scalar_tensor_tensor(trig[:, 0, :, :], trig[:, 1, :, :], -part, trig[:, 0, :, :], ALU.mult, ALU.add))
                settle()
            dve.tensor_scalar(trig[:, 0, :, :], trig[:, 0, :, :], SIN_MAX, -SIN_MAX, ALU.min, ALU.max).then_inc(s_trig, 1)
            dve.wait_ge(s_trig, 1)
            step(dve.scalar_tensor_tensor(trig[:, 1, :, :], trig[:, 0, :, :], -1.0, trig[:, 0, :, :], ALU.mult, ALU.max))
            settle()
            dve.tensor_scalar(trig[:, 1, :, :], trig[:, 1, :, :], -1.0, TWO_PI / 4, ALU.mult, ALU.add).then_inc(s_trig, 1)
            upto(3)
            dve.wait_ge(s_sq, 6)
            step(mean(LAT, 2, B_QL, 2))
            mean(LAT + 1, 2, B_KVL, 2).then_inc(s_ms, 1)
            dve.wait_ge(s_rstd, 2)
            dve.wait_ge(s_small, 48)
            for t in range(TT):
                for i, (c0, c1) in enumerate(((0, B_QL), (B_QL, B_QL + B_KVL))):
                    col = LAT + 2 * t + i
                    dve.scalar_tensor_tensor(lat[:, t, c0:c1], proj[:, t, 1536 + c0:1536 + c1], rstd[:, col:col + 1],
                                             small_g[:, c0:c1], ALU.mult, ALU.mult).then_inc(s_lat, 1)
            upto(5)
            dve.wait_ge(s_hiT, 5)
            dve.tensor_tensor(llo[:, 0:2, :], bank("lat0").rearrange("p (k s) -> p k s", k=2), lhi[:, 0:2, :].bitcast(F),
                              ALU.subtract).then_inc(s_loT, 1)
            dve.wait_ge(s_hiT, 6)
            dve.tensor_tensor(llo[:, 2, :], bank("lat1")[:, 0:S], lhi[:, 2, :].bitcast(F), ALU.subtract).then_inc(s_loT, 1)
            step(dve.tensor_scalar(g_sub, g_sub, 1.0 - LAMBDA_INIT, None, ALU.mult))
            dve.wait_ge(s_lam_in, 64)
            for i in range(2):
                last = dve.tensor_tensor_reduce(out=lam_in[:, 2 * i, :], in0=lam_in[:, 2 * i, :], in1=lam_in[:, 2 * i + 1, :],
                                                scale=1.0, scalar=0.0, op0=ALU.mult, op1=ALU.add, accum_out=lam[:, i:i + 1])
            last.then_inc(s_lam, 1)
            upto(9)
            heads_lo("qA", qA, 2, 0)
            heads_lo("kA", kA, 2, 2)
            upto(11)
            for g in range(4):
                key = ("kB", g)
                wait_full(dve, key)
                dve.tensor_copy(kT[0:B_QK, 2 * g:2 * g + 2, :].rearrange("p k s -> p (k s)"),
                                ps[0:B_QK, use[key][0], :]).then_inc(free[use[key][0]], 1)
            dve.wait_ge(s_bias, 1)

            def maxima(u):
                dve.wait_ge(s_sc, u + 1)
                if u < A_HEADS:
                    if u >= 2:
                        dve.wait_ge(s_exp, u - 1)
                    for (c0, c1) in ((0, 128), (128, 384)):
                        n = c1 - c0
                        step(dve.scalar_tensor_tensor(biased[u % 2][:, c0:c1], ps[:, 2 * (u % 2), c0:c1], A_SCALE,
                                                      bias[:, u, n - 1::-1], ALU.mult, ALU.add))
                    settle()
                maps = 1 if u < UNITS0 else 2
                for m in range(maps):
                    for t, (c0, c1) in enumerate(((0, 128), (128, 384))):
                        col = 2 * m + t
                        src = biased[u % 2][:, c0:c1] if u < A_HEADS else ps[:, 2 * (u % 2) + m, c0:c1]
                        step(dve.reduce_max(mx[:, u, col:col + 1], src, AX.X))
                settle()
                scale = 1.0 if u < A_HEADS else B_SCALE if u < UNITS0 else C_SCALE
                dve.tensor_scalar(nmx[:, u, 0:2 * maps], mx[:, u, 0:2 * maps], -scale, None, ALU.mult).then_inc(s_nm, 1)

            def over_sum(u):
                dve.wait_ge(s_exp, u + 1)
                step(dve.reciprocal(rden[:, u, 0:2], den[:, u, 0:2]))
                settle()
                for t, (c0, c1) in enumerate(((0, 128), (128, 384))):
                    last = dve.tensor_scalar(probs[u % 2][:, c0:c1], probs[u % 2][:, c0:c1], rden[:, u, t:t + 1], None, ALU.mult)
                last.then_inc(s_prn, 1)

            def left1_lo(groups):
                for g in groups:
                    dve.wait_ge(s_hiT, LEFT[1] - 3 + g)
                    dve.tensor_tensor(xlo[:, 2 * g:2 * g + 2, :].rearrange("p k s -> p (k s)"),
                                      xn[:, g // 2, g % 2 * CH:(g % 2 + 1) * CH],
                                      xhi[:, 2 * g:2 * g + 2, :].rearrange("p k s -> p (k s)").bitcast(F),
                                      ALU.subtract).then_inc(s_loT, 1)

            maxima(0)
            maxima(1)
            over_sum(0)
            for u in range(UNITS0):
                if u + 2 < UNITS0:
                    maxima(u + 2)
                if u + 1 < UNITS0:
                    over_sum(u + 1)
                if u == UNITS0 - 1:
                    left1_lo((0, 1, 2))
                dve.wait_ge(s_of, u + 1)
                rows, at = slice(64 * (u % 2), 64 * (u % 2) + 64), u // 2 % 4 * S
                dve.tensor_copy(xn[rows, u // 8, at:at + S], ps[rows, 6 + u % 2, 0:S]).then_inc(s_mix, 1)
            left1_lo((3,))
            upto(13)
            dve.wait_ge(s_used, T_OUT0 + 2)
            add_columns("out0", 0)
            upto(15)
            dve.wait_ge(s_used, T_OUT0 + 4)
            add_columns("out0", 1)
            left_lo(2)
            rstd_of(FFN0)
            upto(T_FFN + 5)

            def hidden(j, width=CH):
                dve.wait_ge(f_act, j + 1)
                for t in range(TT):
                    last = dve.scalar_tensor_tensor(hid[:, t, 0:width], ps[:, 2 + t, 0:width],
                                                    rstd[:, 2 * FFN0 + t:2 * FFN0 + t + 1], act_g[:, t, 0:width],
                                                    ALU.mult, ALU.mult)
                last.then_inc(f_h, 1)

            def hid_lo(j, k=4):
                dve.wait_ge(f_hhi, j + 1)
                dve.tensor_tensor(hidlo[:, 0:k, :], ps[:, 4:6, :].rearrange("p b (k s) -> p (b k) s", k=2)[:, 0:k, :],
                                  hidhi[:, 0:k, :].bitcast(F), ALU.subtract).then_inc(f_ht, 1)

            def add_down(t, half):
                part = h[:, t, half * CH:(half + 1) * CH]
                dve.tensor_tensor(part, part, ps[:, 6 + t, :], ALU.add).then_inc(f_add, 1)

            dve.wait_ge(s_used, T_FFN + 4)
            dve.wait_ge(s_rstd, RSTD[FFN0])
            hidden(0)
            with dve.Fori(1, N_FULL) as j:
                def split_next(r):
                    n = T_FFN + 4 + r
                    dve.wait_ge(s_hi, (j - 1) * 6 + (n + 1))
                    dve.tensor_tensor(wlo[n % SPLIT][:, :], raw[n % RAW][:, :], whi[n % SPLIT][:, :].bitcast(F),
                                      ALU.subtract).then_inc(s_lo, 1)

                split_next(2)
                split_next(3)
                hid_lo(j - 1)
                split_next(4)
                split_next(5)
                dve.wait_ge(s_used, (j - 1) * 6 + (T_FFN + 8))
                hidden(j)
                split_next(6)
                dve.wait_ge(f_d, j * 2 - 1)
                add_down(0, 0)
                dve.wait_ge(s_used, (j - 1) * 6 + (T_FFN + 9))
                add_down(1, 0)
                split_next(7)
                dve.wait_ge(f_d, j * 2)
                add_down(0, 1)
                dve.wait_ge(s_used, (j - 1) * 6 + (T_FFN + 10))
                add_down(1, 1)
            done[0] = T_LAST + 2
            upto(T_LAST + 2)
            hid_lo(LAST - 1)
            upto(T_LAST + 3)
            dve.wait_ge(s_used, T_LAST + 2)
            hidden(LAST, 256)
            for half in range(2):
                upto(T_LAST + 4 + half)
                dve.wait_ge(f_d, 2 * LAST - 1 + half)
                add_down(0, half)
                dve.wait_ge(s_used, T_LAST + 3 + half)
                add_down(1, half)
            hid_lo(LAST, 2)
            upto(T_LAST + 6)
            for i in range(4):
                if i < 3:
                    dve.wait_ge(f_d, 2 * LAST + 1 + i)
                else:
                    dve.wait_ge(s_used, T_LAST + 5)
                add_down(i % 2, i // 2)
            left_lo(3)
            upto(T_IN1 + 2)
            rstd_of(MIX1)

            dve.wait_ge(s_tab, 4)
            for c in range(4):
                if c == 2:
                    upto(T_IN1 + 7)
                    heads_lo("qC", qC, 4, 4)
                upto(T_IN1 + 2 * c + 3)
                dve.wait_ge(s_used, T_IN1 + 2 * c + 2)
                for t in range(TT):
                    key = ("in1", c, t)
                    x = bank(key).rearrange("p (a b) -> p a b", a=8)
                    r0, r1 = [r[:, :].rearrange("p (a b) -> p a b", a=8) for r in rot]
                    step(dve.tensor_tensor(r0, x, spread(cc[:, t, :], [P, 8, C_DH], 1), ALU.mult))
                    step(dve.tensor_tensor(r1[:, :, 0:32], x[:, :, 32:64], spread(ss[:, t, 0:32], [P, 8, 32], 1), ALU.mult))
                    dve.tensor_tensor(r1[:, :, 32:64], x[:, :, 0:32], spread(ss[:, t, 32:64], [P, 8, 32], 1),
                                      ALU.mult).then_inc(free[use[key][0]], 1)
                    settle()
                    wait_free(dve, key)
                    dve.tensor_tensor(rotated[:, t, c % 2 * CH:(c % 2 + 1) * CH], rot[0][:, :], rot[1][:, :],
                                      ALU.add).then_inc(s_rot, 1)
                    dve.wait_ge(s_rot, 2 * c + t + 1)
                if c == 1:
                    dve.wait_ge(s_wr, 1)
                    dve.tensor_tensor(wr2[:, :, N_EXP:], wr[:], wr2[:, :, 0:N_EXP].bitcast(F), ALU.subtract).then_inc(s_wr, 1)
            dve.wait_ge(s_lam, 2)
            step(dve.tensor_tensor(lam[:, 4:5], lam[:, 2:3], lam[:, 3:4], ALU.subtract))
            settle()
            step(dve.tensor_scalar(lam[:, 5:6], lam[:, 4:5], LAMBDA_INIT, None, ALU.add))
            settle()
            upto(T_IN1 + 11)
            heads_lo("kC", kC, 4, 8)
            upto(T_OUT1 + 1)

            def difference(u):
                dve.wait_ge(s_exp, u + 1)
                step(dve.reciprocal(rden[:, u, :], den[:, u, :]))
                settle()
                if u >= UNITS0 + 2:
                    dve.wait_ge(s_ptf, u - 1)
                for t, (c0, c1) in enumerate(((0, 128), (128, 384))):
                    step(dve.tensor_scalar(scaled2[:, c0:c1], probs1[u % 2][:, 1, c0:c1], rden[:, u, 2 + t:3 + t],
                                           lam[:, 5:6], ALU.mult, ALU.mult))
                settle()
                for t, (c0, c1) in enumerate(((0, 128), (128, 384))):
                    last = dve.scalar_tensor_tensor(diff[u % 2][:, c0:c1], probs1[u % 2][:, 0, c0:c1], rden[:, u, t:t + 1],
                                                    scaled2[:, c0:c1], ALU.mult, ALU.subtract)
                last.then_inc(s_diff, 1)
                dve.wait_ge(s_diff, u - UNITS0 + 1)

            maxima(UNITS0)
            maxima(UNITS0 + 1)
            difference(UNITS0)
            for i in range(C_HEADS + 1):
                u = UNITS0 + i
                if u + 2 < UNITS:
                    maxima(u + 2)
                if u + 1 < UNITS:
                    difference(u + 1)
                if u < UNITS:
                    dve.wait_ge(s_of, u + 1)
                    dve.tensor_copy(xn[:, :, i * C_DV:(i + 1) * C_DV],
                                    ps[:, 6 + u % 2, 0:2 * C_DV].rearrange("p (t d) -> p t d", t=TT)).then_inc(s_mix, 1)
                if 0 <= i - 1 < C_HEADS:
                    dve.wait_ge(s_sqc, i)
                    mean(SUBLN + i - 1, TT, C_DV, C_HEADS).then_inc(s_ms, 1)
                if 0 <= i - 4 < C_HEADS - 3:
                    dve.wait_ge(c_hi, i - 3)
                    dve.tensor_tensor(xlo[:, i - 4, :], ps[:, 6 + (u - 1) % 2, S:2 * S], xhi[:, i - 4, :].bitcast(F),
                                      ALU.subtract).then_inc(c_lo, 1)
            for i, n in enumerate((2, 1)):
                dve.wait_ge(c_hi, C_HEADS - 2 + i)
                blocks = slice(C_HEADS - 3 + 2 * i, C_HEADS - 3 + 2 * i + n)
                dve.tensor_tensor(xlo[:, blocks, :].rearrange("p k s -> p (k s)"), ps[:, 4 + i, 0:n * S],
                                  xhi[:, blocks, :].rearrange("p k s -> p (k s)").bitcast(F), ALU.subtract).then_inc(c_lo, 1)
            upto(T_OUT1 + 3)
            dve.wait_ge(s_used, T_OUT1 + 2)
            add_columns("out1", 0)
            upto(T_MOE + 1)
            dve.wait_ge(s_used, T_OUT1 + 4)
            add_columns("out1", 1)
            left_lo(5)
            rstd_of(FFN1)

            def grid(x):
                return spread(x, [P, TT, 8], 2)

            def over_tiles(x):
                return spread(x, [P, TT, 8], 1)

            dve.wait_ge(s_logT, 1)
            dve.tensor_copy(logT[:], ps[0:2 * N_EXP, 0, 0:S]).then_inc(s_logS, 1)
            norm(FFN1, 0, s_xn)
            dve.wait_ge(s_log, 1)
            for t in range(TT):
                step(dve.tensor_scalar(logit[:, t, :], ps[:, 0, S + 8 * t:S + 8 * t + 8], rstd[:, 2 * FFN1 + t:2 * FFN1 + t + 1], None,
                                       ALU.mult))
            settle()
            src = logit
            for i in range(2):
                step(dve.reduce_max(rs[:, 2 * i, :], src[:] if i == 0 else rt[:, 0, :, :], AX.X))
                settle()
                step(dve.tensor_tensor(rt[:, 1, :, :], src[:] if i == 0 else rt[:, 0, :, :], grid(rs[:, 2 * i, :]), ALU.is_equal))
                settle()
                step(dve.tensor_tensor(rt[:, 1, :, :], rt[:, 1, :, :], over_tiles(r8), ALU.mult))
                settle()
                step(dve.reduce_max(rs[:, 2 * i + 1, :], rt[:, 1, :, :], AX.X))
                settle()
                step(dve.tensor_tensor(rt[:, 2 + i, :, :], rt[:, 1, :, :], grid(rs[:, 2 * i + 1, :]), ALU.is_equal))
                settle()
                if i == 0:
                    step(dve.scalar_tensor_tensor(rt[:, 0, :, :], rt[:, 2, :, :], -3.0e38, logit[:], ALU.mult, ALU.add))
                    settle()
            dve.tensor_tensor(rs[:, 4, :], rs[:, 2, :], rs[:, 0, :], ALU.subtract).then_inc(s_dlt, 1)
            dve.tensor_tensor(chosen[:, :, 0:8], rt[:, 2, :, :], rt[:, 3, :, :], ALU.add).then_inc(s_cho, 1)
            dve.wait_ge(s_ex, 1)
            step(dve.tensor_scalar(rs[:, 6, :], rs[:, 5, :], 1.0, None, ALU.add))
            settle()
            step(dve.reciprocal(rs[:, 7, :], rs[:, 6, :]))
            settle()
            step(dve.tensor_tensor(rs[:, 8, :], rs[:, 5, :], rs[:, 7, :], ALU.mult))
            settle()
            step(dve.tensor_tensor(rt[:, 4, :, :], rt[:, 2, :, :], grid(rs[:, 7, :]), ALU.mult))
            step(dve.tensor_tensor(rt[:, 5, :, :], rt[:, 3, :, :], grid(rs[:, 8, :]), ALU.mult))
            settle()
            step(dve.tensor_tensor(gate[:, :, 0:8], rt[:, 4, :, :], rt[:, 5, :, :], ALU.add))
            def select(p):
                dve.tensor_copy(gcur[:], gate[:, :, ds(p, 1)].rearrange("p t o -> p (t o)"))
                for t in range(TT):
                    last = dve.tensor_scalar(sel[:, t, :], iota, slot[:, t, ds(p, 1)], chosen[:, t, ds(p, 1)],
                                             ALU.is_equal, ALU.mult)
                last.then_inc(m_sel, 1)

            step(dve.memset(scan[:], 0.0))
            for table in (chosen, slot, gate):
                step(dve.memset(table[:, :, MAX_PASS:], 0.0))
            settle()
            dve.wait_ge(s_rank, 1)
            step(dve.tensor_copy(slot[:, :, 0:8], ps[:, 1, 0:16].rearrange("p (t e) -> p t e", t=TT)))
            step(dve.tensor_scalar(scan[:, 0, 8:16], ps[:, 1, 16:24], float(P), None, ALU.is_gt))
            settle()
            select(0)
            upto(T_MOE + 2)
            def gathered_lo(p):
                dve.wait_ge(m_xhi, p + 1)
                dve.tensor_tensor(xglo[:], ps[:, 6:8, :].rearrange("p b (k s) -> p (b k) s", k=4), xghi[:].bitcast(F),
                                  ALU.subtract).then_inc(m_xlo, 1)

            def output_lo(p):
                dve.wait_ge(m_yhi, p + 1)
                dve.wait_ge(m_auxr, p + 1)
                dve.scalar_tensor_tensor(ylo[:], ps[:, 3:5, :].rearrange("p b n -> p (b n)"), gslot[:, 0:1],
                                         yhi[:].bitcast(F), ALU.mult, ALU.subtract).then_inc(m_ylo, 1)

            def add_back(p, t):
                for half in range(2):
                    dve.wait_ge(m_acc, p * 4 + (2 * t + half + 1))
                    part = h[:, t, half * CH:(half + 1) * CH]
                    dve.tensor_tensor(part, part, ps[:, 6 + half, :], ALU.add).then_inc(m_add, 1)

            def expert_pass(p, first):
                def split_tile(i, turns=0, beside=False):
                    n = T_MOE + i
                    src = ahead[i - 9] if beside and i >= 9 else raw[n % RAW]
                    dve.wait_ge(s_hi, p * M_TILES + turns * 6 + (n + 1))
                    dve.tensor_tensor(wlo[n % SPLIT][:, :], src[:, :], whi[n % SPLIT][:, :].bitcast(F),
                                      ALU.subtract).then_inc(s_lo, 1)

                def hidden_e(j):
                    dve.wait_ge(m_act, p * M_CH + j + 1)
                    dve.tensor_tensor(hid_e[:], act_e[:], ps[:, 1, :], ALU.mult).then_inc(m_h, 1)

                def hid_lo_e(j):
                    dve.wait_ge(m_thi, p * M_CH + j + 1)
                    dve.tensor_tensor(helo[:], ps[:, 2, :].rearrange("p (k s) -> p k s", k=4), hehi[:].bitcast(F),
                                      ALU.subtract).then_inc(m_tr, 1)

                if not first:
                    for i in range(3):
                        split_tile(i)
                    output_lo(p - 1)
                split_tile(3)
                if not first:
                    add_back(p - 1, 0)
                split_tile(4)
                split_tile(5)
                dve.wait_ge(s_used, p * M_TILES + (T_MOE + 4))
                hidden_e(0)
                if not first:
                    add_back(p - 1, 1)
                dve.wait_ge(m_aux, p + 1)
                dve.tensor_copy(selT[:], ps[:, 5, 0:S])
                dve.tensor_copy(gslot[:], ps[:, 5, S:S + 1]).then_inc(m_auxr, 1)
                select(p + 1)
                def turn(j, turns, beside=False):
                    split_tile(6, turns)
                    split_tile(7, turns)
                    hid_lo_e(j - 1)
                    split_tile(8, turns)
                    split_tile(9, turns, beside)
                    dve.wait_ge(s_used, p * M_TILES + j * 6 + (T_MOE + 2))
                    hidden_e(j)
                    split_tile(10, turns, beside)
                    split_tile(11, turns, beside)

                if first:
                    turn(1, 0, True)
                with dve.Fori(2 if first else 1, M_CH) as j:
                    turn(j, j - 1)
                hid_lo_e(M_CH - 1)
                gathered_lo(p + 1)

            gathered_lo(0)
            for i, shift in enumerate((1, 2, 4)):
                step(dve.tensor_tensor(scan[:, i + 1, 8:16], scan[:, i, 8:16], scan[:, i, 8 - shift:16 - shift], ALU.add))
                settle()
            step(dve.tensor_copy(order[:, 0:8], e8))
            step(dve.memset(order[:, 11:15], 0.0))
            step(dve.tensor_scalar(order[:, 15:16], scan[:, 3, 15:16], float(N_EXP), None, ALU.add))
            for q in range(MAX_PASS - N_EXP):
                step(dve.scalar_tensor_tensor(rt[:, 6, 0, :], scan[:, 3, 8:16], q + 1.0, scan[:, 0, 8:16], ALU.is_equal, ALU.mult))
                settle()
                step(dve.tensor_tensor(rt[:, 6, 1, :], rt[:, 6, 0, :], e8, ALU.mult))
                for i, table in enumerate((chosen, slot, gate)):
                    step(dve.tensor_tensor(rt[:, 7 + i, :, :], table[:, :, 0:8], over_tiles(rt[:, 6, 0, :]), ALU.mult))
                settle()
                step(dve.reduce_sum(order[:, 8 + q:9 + q], rt[:, 6, 1, :], AX.X))
                step(dve.reduce_sum(chosen[:, :, 8 + q], rt[:, 7, :, :], AX.X))
                step(dve.reduce_sum(rs[:, 9, :], rt[:, 8, :, :], AX.X))
                step(dve.reduce_sum(gate[:, :, 8 + q], rt[:, 9, :, :], AX.X))
                settle()
                step(dve.tensor_scalar(slot[:, :, 8 + q], rs[:, 9, :], -float(P), None, ALU.add))
            settle()
            dve.tensor_copy(order_i[:], order[:]).then_inc(s_order, 1)
            expert_pass(0, True)
            dve.wait_ge(s_order, 1)
            passes = dve.value_load(order_i[0:1, 15:16], min_val=N_EXP, max_val=MAX_PASS)
            with dve.Fori(1, passes) as p:
                expert_pass(p, False)
            dve.wait_ge(m_auxr, passes * 1)
            for half in range(2):
                dve.wait_ge(last_hi, half + 1)
                cols = slice(half * CH, (half + 1) * CH)
                dve.scalar_tensor_tensor(ylo[:, cols], ps[:, 3 + half, :], gslot[:, 0:1], yhi[:, cols].bitcast(F),
                                         ALU.mult, ALU.subtract).then_inc(last_lo, 1)
            for i in range(4):
                half, t = i // 2, i % 2
                dve.wait_ge(last_acc, i + 1)
                part = h[:, t, half * CH:(half + 1) * CH]
                dve.tensor_tensor(part, part, ps[:, LAST_BANKS[i], :], ALU.add).then_inc(last_add, 1)
            rstd_of(FINAL)
            norm(FINAL, 1, s_fin)

        @block.tensor
        def _(pe):
            def three(out, left, right, start, stop):
                for i, (l, r) in enumerate(((0, 0), (0, 1), (1, 0))):
                    last = pe.matmul(out, left[l], right[r], start=start and i == 0, stop=stop and i == 2)
                return last

            def tile(n, k, m):
                return [w[n % SPLIT][:, 0:k * m].rearrange("p (k m) -> p k m", k=k) for w in (whi, wlo)]

            def acquire(key):
                if use[key][2]:
                    pe.wait_ge(free[use[key][0]], use[key][2])

            def keep_warm(n, b):
                for _ in range(n):
                    pe.matmul(ps[:, b, :].rearrange("p (a m) -> p a m", a=4), ident_r[:], spread(ident_r[:], [P, 4, P], 1),
                              start=True, stop=True)

            def halves(stage):
                return s_loT, LEFT[stage] - 2, LEFT[stage]

            def all_read(counts, banks):
                for b in banks:
                    if counts[b]:
                        pe.wait_ge(free[b], counts[b])

            def transposes(key, blocks):
                acquire(key)
                for i, src in enumerate(blocks):
                    m = src.shape[1]
                    last = pe.transpose(ps[0:m, use[key][0], i * P:(i + 1) * P], src, ident)
                last.then_inc(full[use[key][0]], 1)

            def left_operand(stage, src, source=None, counts=()):
                for g in range(4):
                    if g % 2 == 0 and counts:
                        pe.wait_ge(source, counts[g // 2])
                    key = ("left", stage, g)
                    for i, (k, t) in enumerate(((2 * g, 0), (2 * g, 1), (2 * g + 1, 0), (2 * g + 1, 1))):
                        last = pe.transpose(ps[:, use[key][0], i * P:(i + 1) * P], src[:, t, k * P:(k + 1) * P], ident)
                    last.then_inc(full[use[key][0]], 1)

            def columns(stage, c, n, width=CH, left=None, between=None):
                for t in range(TT):
                    acquire((stage, c, t))
                for b in range(2):
                    if b and between:
                        between()
                    if left:
                        pe.wait_ge(left[0], left[1 + b])
                    pe.wait_ge(s_lo, n + b + 1)
                    w = tile(n + b, 4, width)
                    for t in range(TT):
                        for k in range(4):
                            kb = 4 * b + k
                            last = three(bank((stage, c, t))[:, 0:width],
                                         [x[:, kb, t * P:(t + 1) * P] for x in (xhi, xlo)],
                                         [x[:, k, :] for x in w], kb == 0, kb == KB - 1)
                    last.then_inc(s_used, 1)

            pe.wait_ge(s_consts, 16)
            pe.wait_ge(s_rows, 32)
            pe.transpose(ps[:, 0, 0:4 * KB], gain_rows[:, :], ident[0:4 * KB, 0:4 * KB]).then_inc(s_gfull, 1)
            pe.wait_ge(s_x, 16 * TT)
            left_operand(0, h)
            pe.wait_ge(s_fr, 1)
            keep_warm(6, 3)
            pe.wait_ge(s_gT, 1)
            columns("in0", 3, T_IN0, 416, left=halves(0))
            columns("in0", 0, T_IN0 + 2)
            pe.wait_ge(s_lat, 4)
            transposes("lat0", [lat[:, t, k * P:(k + 1) * P] for k in range(2) for t in range(TT)])
            transposes("lat1", [lat[:, t, B_QL:B_QL + B_KVL] for t in range(TT)])
            columns("in0", 1, T_IN0 + 4)
            pe.wait_ge(s_loT, 6)
            pe.wait_ge(s_lo, T_UQ + 1)
            w = tile(T_UQ, 2, 768)
            for c, width in ((0, CH), (1, 768 - CH)):
                for t in range(TT):
                    acquire(("uq", c, t))
                    for k in range(2):
                        last = three(bank(("uq", c, t))[:, 0:width], [x[:, k, t * P:(t + 1) * P] for x in (lhi, llo)],
                                     [x[:, k, c * CH:c * CH + width] for x in w], k == 0, k == 1)
            last.then_inc(s_used, 1)
            pe.wait_ge(s_lo, T_UKV + 1)
            w = tile(T_UKV, 1, D)
            for c in range(2):
                for t in range(TT):
                    acquire(("ukv", c, t))
                    last = three(bank(("ukv", c, t)), [x[:, 2, t * P:(t + 1) * P] for x in (lhi, llo)],
                                 [x[:, 0, c * CH:(c + 1) * CH] for x in w], True, True)
            last.then_inc(s_used, 1)
            for name, c in (("qA", 0), ("kA", 1)):
                for t in range(TT):
                    wait_free(pe, ("in0", c, t))
                for g in range(2):
                    transposes((name, g), [proj[:, t, c * CH + k * P:c * CH + (k + 1) * P]
                                           for k in (2 * g, 2 * g + 1) for t in range(TT)])
            columns("in0", 2, T_IN0V)
            pe.wait_ge(s_rope, 8)
            for t in range(TT):
                for c in range(2):
                    wait_free(pe, ("ukv", c, t))
            for name, src in (("qB", qB), ("kB", kB)):
                for g in range(4):
                    transposes((name, g), [src[:, t, hd, :] for hd in (2 * g, 2 * g + 1) for t in range(TT)])

            def scores(u):
                if u >= 2:
                    pe.wait_ge(s_exp, u - 1)
                for m in range(1 if u < UNITS0 else 2):
                    if u < A_HEADS:
                        rows = slice(64 * (u % 2), 64 * (u % 2) + 64)
                        q, k = [x[rows, u // 2, :] for x in qA], [x[rows, u // 2, :] for x in kA]
                    elif u < UNITS0:
                        q, k = qT[0:B_QK, u - A_HEADS, :], kT[0:B_QK, u - A_HEADS, :]
                    else:
                        rows = slice(64 * m, 64 * m + 64)
                        q, k = [x[rows, u - UNITS0, :] for x in qC], [x[rows, u - UNITS0, :] for x in kC]
                    b = 2 * (u % 2) + m
                    masked = u >= A_HEADS
                    for t in range(TT):
                        c0, c1 = ((0, 128), (128, 384))[t]
                        out = ps[:, b, c0:c1]
                        if A_HEADS <= u < UNITS0:
                            pe.matmul(out, q[:, t * P:(t + 1) * P], k[:, 0:c1 - c0], start=t == 0, stop=False)
                        else:
                            last = three(out, [x[:, t * P:(t + 1) * P] for x in q], [x[:, 0:c1 - c0] for x in k],
                                         t == 0 or not masked, not masked)
                    if masked:
                        last = pe.matmul(ps[:, b, 0:CH].rearrange("p (t c) -> p t c", t=TT)[:, :, 64:128], ident_r[:],
                                         spread(mask_r[:], [P, TT, 64], 1), start=False, stop=True)
                last.then_inc(s_sc, 1)

            def headT(hd, b, at):
                pe.wait_ge(s_sub, hd + 1)
                for t in range(TT):
                    last = pe.transpose(ps[:, b, at + t * P:at + (t + 1) * P], xn[:, t, hd * C_DV:(hd + 1) * C_DV], ident)
                return last

            def unit(u, src, value, ready, count, last_unit):
                idle = 4 + (u + 1) % 2
                if u in (0, UNITS0):
                    keep_warm(WARM_FIRST, idle)
                if u + 2 < last_unit:
                    scores(u + 2)
                keep_warm(WARM_PROBS[u > UNITS0], idle)
                pe.wait_ge(ready, count)
                if u >= 2:
                    pe.wait_ge(s_pT, u - 1)
                for i in range(3):
                    last = pe.transpose(ps[:, 4 + u % 2, i * P:(i + 1) * P], src[:, i * P:(i + 1) * P], ident)
                last.then_inc(s_ptf, 1)
                if u:
                    keep_warm(WARM_T, idle)
                if u < UNITS0 + 3:
                    pe.wait_ge(s_pT, u + 1)
                if u >= 2:
                    pe.wait_ge(s_mix, u - 1)
                if u >= UNITS0 + 3:
                    if u >= UNITS0 + 5:
                        pe.wait_ge(c_lo, u - UNITS0 - 4)
                    headT(u - UNITS0 - 3, 6 + u % 2, S)
                    pe.wait_ge(s_pT, u + 1)
                out = ps[:, 6 + u % 2, :]
                dst = probsT if u < UNITS0 else diffT
                if u < UNITS0:
                    out = out[64 * (u % 2):64 * (u % 2) + 64, :]
                    pe.matmul(out[:, 0:S], value(0), dst[u % 2][:, 0:S], start=True, stop=False)
                    pe.matmul(out[:, P:S], value(1), dst[u % 2][:, S:S + P], start=False, stop=True).then_inc(s_of, 1)
                    return
                pe.matmul(out[:, 0:C_DV], dst[u % 2][:, 0:P], value(0), start=True, stop=True)
                pe.matmul(out[:, C_DV:2 * C_DV], dst[u % 2][:, P:2 * P], value(0), start=True, stop=False)
                pe.matmul(out[:, C_DV:2 * C_DV], dst[u % 2][:, 2 * P:3 * P], value(1), start=False, stop=True)\
                    .then_inc(s_of, 1)

            all_read(before_units0, range(4))
            scores(0)
            scores(1)
            all_read(before_units0, range(4, 8))
            for u in range(UNITS0):
                def value(t):
                    return proj[:, t, 1024 + 64 * u:1088 + 64 * u] if u < A_HEADS else vB[:, t, u - A_HEADS, :]
                unit(u, probs[u % 2], value, s_prn, u + 1, UNITS0)
            for c in range(2):
                columns("out0", c, T_OUT0 + 2 * c, left=None if c else halves(1))
            left_operand(2, h, s_res, (2, 4))
            def dense(n, b, first, width=CH, kb=4):
                w = tile(n, kb, width)
                for t in range(TT):
                    for k in range(kb):
                        last = three(ps[:, b + t, 0:width], [x[:, first + k, t * P:(t + 1) * P] for x in (xhi, xlo)],
                                     [x[:, k, :] for x in w], first + k == 0, first + k == KB - 1)
                last.then_inc(s_used, 1)

            def hid_transposes(j, k=4):
                pe.wait_ge(f_h, j + 1)
                for i in range(k):
                    for t in range(TT):
                        at = (2 * (i % 2) + t) * P
                        last = pe.transpose(ps[:, 4 + i // 2, at:at + P], hid[:, t, i * P:(i + 1) * P], ident)
                last.then_inc(f_t, 1)

            for r in range(4):
                if r < 2:
                    pe.wait_ge(s_loT, LEFT[2] - 2 + 2 * r)
                pe.wait_ge(s_lo, T_FFN + r + 1)
                dense(T_FFN + r, 2 * (r // 2), 4 * (r % 2))
            with pe.Fori(1, N_FULL) as j:
                for r in range(6):
                    n = T_FFN + 4 + r
                    if r == 0:
                        pe.wait_ge(f_act, j * 1)
                    if r == 2:
                        hid_transposes(j - 1)
                    if r == 4:
                        pe.wait_ge(f_ht, j * 1)
                    pe.wait_ge(s_lo, (j - 1) * 6 + (n + 1))
                    if r < 4:
                        dense(n, 2 * (r // 2), 4 * (r % 2))
                    else:
                        w = tile(n, 4, CH)
                        for t in range(TT):
                            if r == 5:
                                pe.wait_ge(f_add, (j - 1) * 4 + 1 + t)
                            for k in range(4):
                                last = three(ps[:, 6 + t, :], [x[:, k, t * P:(t + 1) * P] for x in (hidhi, hidlo)],
                                             [x[:, k, :] for x in w], k == 0, k == 3)
                            last.then_inc(f_d if t == 0 else s_used, 1)
            pe.wait_ge(f_act, LAST)
            pe.wait_ge(s_lo, T_LAST + 1)
            dense(T_LAST, 0, 0, 256, KB)
            hid_transposes(LAST - 1)
            pe.wait_ge(s_lo, T_LAST + 2)
            dense(T_LAST + 1, 2, 0, 256, KB)
            pe.wait_ge(f_ht, LAST)
            for half in range(2):
                n = T_LAST + 2 + half
                pe.wait_ge(s_lo, n + 1)
                w = tile(n, 4, CH)
                for t in range(TT):
                    pe.wait_ge(f_add, 4 * (LAST - 1) + (1 + t if half else 0))
                    for k in range(4):
                        last = three(ps[:, 6 + t, :], [x[:, k, t * P:(t + 1) * P] for x in (hidhi, hidlo)],
                                     [x[:, k, :] for x in w], k == 0, k == 3)
                    last.then_inc(f_d if t == 0 else s_used, 1)
            hid_transposes(LAST, 2)
            pe.wait_ge(f_ht, LAST + 1)
            pe.wait_ge(s_lo, T_LAST + 5)
            w = tile(T_LAST + 4, 2, D)
            for i in range(4):
                half, t = i // 2, i % 2
                pe.wait_ge(f_add, 4 * LAST + i - 1)
                for k in range(2):
                    last = three(ps[:, 6 + t, :], [x[:, k, t * P:(t + 1) * P] for x in (hidhi, hidlo)],
                                 [x[:, k, half * CH:(half + 1) * CH] for x in w], k == 0, k == 1)
                last.then_inc(f_d if i < 3 else s_used, 1)

            left_operand(3, h, f_add, (4 * LAST + 2, 4 * LAST + 4))
            for c in range(6):
                columns("in1", c, T_IN1 + 2 * c, left=None if c else halves(3))
                if c in (2, 4):
                    name, c0 = ("qC", 0) if c == 2 else ("kC", 2)
                    pe.wait_ge(s_rot, 2 * c0 + 4)
                    for g in range(4):
                        transposes((name, g), [rotated[:, t, k * P:(k + 1) * P]
                                               for k in (2 * g, 2 * g + 1) for t in range(TT)])
            all_read(before_units1, (0, 1, 4, 5, 6, 7))
            scores(UNITS0)
            all_read(before_units1, (2, 3))
            scores(UNITS0 + 1)
            for u in range(UNITS0, UNITS):
                def value(t):
                    return vC[:, t, C_DV * (u - UNITS0):C_DV * (u - UNITS0 + 1)]
                unit(u, diff[u % 2], value, s_diff, u - UNITS0 + 1, UNITS)

            def last_heads():
                pe.wait_ge(s_pT, UNITS)
                headT(C_HEADS - 3, 4, 0)
                headT(C_HEADS - 2, 4, S).then_inc(c_t, 1)
                headT(C_HEADS - 1, 5, 0).then_inc(c_t, 1)

            for c in range(2):
                if c == 0:
                    columns("out1", c, T_OUT1, left=(c_lo, C_HEADS // 2, C_HEADS - 1), between=last_heads)
                else:
                    columns("out1", c, T_OUT1 + 2)
            left_operand(5, h, s_res, (6, 8))
            pe.wait_ge(s_wr, 2)
            for k in range(KB):
                if k % 2 == 0:
                    pe.wait_ge(s_loT, LEFT[5] - 3 + k // 2)
                for i, x in enumerate((xhi, xlo)):
                    last = pe.matmul(ps[0:2 * N_EXP, 0, 0:S], wr2[:, k, :], x[:, k, :], start=k == 0 and i == 0,
                                     stop=k == KB - 1 and i == 1)
            last.then_inc(s_logT, 1)
            keep_warm(2, 2)
            pe.wait_ge(s_logS, 1)
            for t in range(TT):
                last = pe.matmul(ps[:, 0, S + 8 * t:S + 8 * t + 8], logT[:, t * P:(t + 1) * P], fold, start=True, stop=True)
            last.then_inc(s_log, 1)
            keep_warm(22, 2)
            pe.wait_ge(s_cho, 1)
            pe.matmul(ps[:, 1, 0:8], tri, chosen[:, 0, 0:8], start=True, stop=True)
            pe.matmul(ps[:, 1, 8:16], ones, chosen[:, 0, 0:8], start=True, stop=False)
            pe.matmul(ps[:, 1, 8:16], tri, chosen[:, 1, 0:8], start=False, stop=True)
            pe.matmul(ps[:, 1, 16:24], ones, chosen[:, 0, 0:8], start=True, stop=False)
            pe.matmul(ps[:, 1, 16:24], ones, chosen[:, 1, 0:8], start=False, stop=True).then_inc(s_rank, 1)

            def gather(p):
                pe.wait_ge(m_sel, p + 1)
                for k in range(KB):
                    for t in range(TT):
                        for i, x in enumerate((thi, tlo)):
                            last = pe.matmul(ps[:, 6 + k // 4, (k % 4) * P:(k % 4 + 1) * P], x[:, t, k * P:(k + 1) * P],
                                             sel[:, t, :], start=t == 0 and i == 0, stop=t == 1 and i == 1)
                last.then_inc(m_x, 1)

            def scatter(p, t):
                for half in range(2):
                    if t:
                        pe.wait_ge(m_add, p * 4 + (half + 1))
                    for n, y in enumerate((yhi, ylo)):
                        last = pe.matmul(ps[:, 6 + half, :], selT[:, t * P:(t + 1) * P], y[:, half * CH:(half + 1) * CH],
                                         start=n == 0, stop=n == 1)
                    last.then_inc(m_acc, 1)

            def expert_pass(p, first):
                def ready(i, turns=0):
                    pe.wait_ge(s_lo, p * M_TILES + turns * 6 + (T_MOE + i + 1))

                def expert(i, b, first_block):
                    w = tile(T_MOE + i, 4, CH)
                    for k in range(4):
                        kb = first_block + k
                        last = three(ps[:, b, :], [xghi[:, kb, :], xglo[:, kb, :]], [x[:, k, :] for x in w],
                                     kb == 0, kb == KB - 1)
                    last.then_inc(s_used, 1)

                def hid_transposes_e(j):
                    pe.wait_ge(m_h, p * M_CH + j + 1)
                    for i in range(4):
                        last = pe.transpose(ps[:, 2, i * P:(i + 1) * P], hid_e[:, i * P:(i + 1) * P], ident)
                    last.then_inc(m_t, 1)

                def down_e(i, half, start, stop):
                    w = tile(T_MOE + i, 4, CH)
                    for k in range(4):
                        last = three(ps[:, 3 + half, :], [hehi[:, k, :], helo[:, k, :]], [x[:, k, :] for x in w],
                                     start and k == 0, stop and k == 3)
                    last.then_inc(s_used, 1)

                def turn(j, start, turns):
                    for r in range(6):
                        if r == 0:
                            pe.wait_ge(m_act, p * M_CH + j)
                        if r == 2:
                            hid_transposes_e(j - 1)
                        if r == 4:
                            pe.wait_ge(m_tr, p * M_CH + j)
                        ready(4 + r, turns)
                        if r < 4:
                            expert(4 + r, r // 2, 4 * (r % 2))
                        else:
                            down_e(4 + r, r - 4, start, False)

                pe.wait_ge(m_xlo, p + 1)
                for i in range(4):
                    ready(i)
                    expert(i, i // 2, 4 * (i % 2))
                    if i % 2 and not first:
                        if i == 1:
                            pe.wait_ge(m_ylo, p * 1)
                        scatter(p - 1, i // 2)
                for t in range(TT):
                    pe.transpose(ps[:, 5, t * P:(t + 1) * P], sel[:, t, :].bitcast(F), ident)
                for t in range(TT):
                    last = pe.matmul(ps[:, 5, S:S + 1], sel[:, t, :].bitcast(F), gcur[:, t:t + 1], start=t == 0, stop=t == 1)
                last.then_inc(m_aux, 1)
                turn(1, True, 0)
                with pe.Fori(2, M_CH) as j:
                    turn(j, False, j - 1)
                hid_transposes_e(M_CH - 1)
                gather(p + 1)
                pe.wait_ge(m_tr, p * M_CH + M_CH)
                for half in range(2):
                    ready(M_TILES - 2 + half)
                    down_e(M_TILES - 2 + half, half, False, True)

            keep_warm(5, 2)
            pe.wait_ge(s_tlo, TT)
            gather(0)
            keep_warm(8, 2)
            expert_pass(0, True)
            pe.wait_ge(s_order, 1)
            passes = pe.value_load(order_i[0:1, 15:16], min_val=N_EXP, max_val=MAX_PASS)
            with pe.Fori(1, passes) as p:
                expert_pass(p, False)
            for i in range(4):
                half, t = i // 2, i % 2
                pe.wait_ge(last_lo, half + 1)
                for n, y in enumerate((yhi, ylo)):
                    last = pe.matmul(ps[:, LAST_BANKS[i], :], selT[:, t * P:(t + 1) * P], y[:, half * CH:(half + 1) * CH],
                                     start=n == 0, stop=n == 1)
                last.then_inc(last_acc, 1)


_INS = ["x", "positions", "mix_norm_g", "ffn_norm_g", "w_in_even", "rel_bias_a", "q_norm_b", "w_uq_b", "kv_norm_b",
        "w_ukv_b", "w_out_even", "w_in_odd", "lambda_q1", "lambda_k1", "lambda_q2", "lambda_k2", "subln_g",
        "w_out_odd", "w_gu_dense", "w_down_dense", "w_router", "w_gu_moe", "w_down_moe", "final_norm_g"]


def constants():
    c = np.zeros((P, C_COLS), np.float32)
    c[:, C_ID:C_ID + P] = np.eye(P)
    c[:, C_TRI:C_TRI + P] = np.triu(np.ones((P, P)), 1)
    c[:, C_ONES:C_ONES + P] = 1.0
    c[:, C_IOTA:C_IOTA + P] = np.arange(P)
    c[0:64, C_MASK:C_MASK + 64] = NEG
    at = C_FREQ
    for dim in (B_ROPE, C_DH):
        power = np.power(np.float32(10000.0), np.arange(0, dim, 2, dtype=np.float32) / np.float32(dim))
        c[:, at:at + dim // 2] = np.float32(1.0) / power
        at += dim // 2
    c[:, C_E8:C_E8 + 8] = np.arange(8)
    c[:, C_R8:C_R8 + 8] = 8 - np.arange(8)
    c[0:2 * N_EXP, C_FOLD:C_FOLD + 8] = np.concatenate([np.eye(N_EXP), np.eye(N_EXP)])
    return c


def kernel(**inputs):
    import concourse.bacc as bacc
    from concourse.bass_utils import run_bass_kernel_spmd

    nc = bacc.Bacc("TRN2", target_bir_lowering=False, num_devices=1)
    arrays, aps = {}, {}
    for name in _INS:
        arrays[name] = np.ascontiguousarray(inputs[name])
    arrays["consts"] = constants()
    for name, v in arrays.items():
        aps[name] = nc.dram_tensor(name, v.shape, mybir.dt.from_np(v.dtype), kind="ExternalInput").ap()
    aps["out"] = nc.dram_tensor("out", (1, S, D), mybir.dt.float32, kind="ExternalOutput").ap()
    build(nc, aps)
    r = run_bass_kernel_spmd(nc, [arrays], core_ids=[0])
    return r.results[0]["out"]
```
